# Optimizing a Trainium2 kernel written in Bass

```python
import math
import jax, jax.numpy as jnp
from jax import lax
import numpy as np

D_MODEL = 1024
BATCH = 1
SEQ = 512
DEPTH = 4
DEC_BATCH = 8
DEC_SEQ = 1
PAST_LEN = 256
PAGE_SIZE = 128

N_MIXERS = 3
N_A = (DEPTH + 2) // 3
N_B = (DEPTH + 1) // 3
N_C = DEPTH // 3

HG_HEADS = 8
HG_DK = 128
HG_DV = D_MODEL // HG_HEADS
HG_F = HG_HEADS * HG_DK
HG_CHUNK = 32
HG_IN = 2 * HG_F + 2 * D_MODEL

AT_HEADS = 8
AT_DH = D_MODEL // AT_HEADS
IDX_HEADS = 8
IDX_DIM = 64
TOPK_MAX = 256
Q_BLOCK = 128
REL_BUCKETS = 32
REL_MAX_DIST = 128
DSA_IN = 3 * AT_HEADS * AT_DH + IDX_HEADS * IDX_DIM + IDX_DIM + IDX_HEADS
NEG_BIG = -1e30

S5_GROUP = 16
S5_GROUPS = D_MODEL // S5_GROUP
S5_STATE = 64
S5_DT_MIN = 1e-3
S5_DT_MAX = 1e-1

FFN_HIDDEN = 4 * D_MODEL
DN_ALPHA = (2 * DEPTH) ** 0.25
DN_BETA = (8 * DEPTH) ** -0.25
LN_EPS = 1e-5
RMS_EPS = 1e-6

kernel_name = 'hgrn2_dsa_s5_hybrid_decode_step'

def layer_norm(x, g, b):
    xf = x.astype(jnp.float32)
    mu = jnp.mean(xf, -1, keepdims=True)
    var = jnp.mean(jnp.square(xf - mu), -1, keepdims=True)
    return ((xf - mu) * lax.rsqrt(var + LN_EPS) * g + b).astype(x.dtype)

def sq_relu_mlp(x, w1, w2):
    return jnp.square(jax.nn.relu(x @ w1)) @ w2

def hgrn2_chunk_scan(q, k, v, logf, s0):
    n, l = q.shape[:2]
    c = min(HG_CHUNK, l)
    pad = (-l) % c
    if pad:
        padw = ((0, 0), (0, pad), (0, 0), (0, 0))
        q, k, v, logf = [jnp.pad(a, padw) for a in (q, k, v, logf)]
    nc = (l + pad) // c

    def to_chunks(a):
        return a.reshape(n, nc, c, a.shape[2], a.shape[3]).transpose(1, 0, 3, 2, 4)

    causal = jnp.tril(jnp.ones((c, c), bool))[:, :, None]

    def step(s, inp):
        qc, kc, vc, gc = inp
        b = jnp.cumsum(gc, axis=2)
        diff = b[:, :, :, None, :] - b[:, :, None, :, :]
        decay = jnp.where(causal, jnp.exp(jnp.where(causal, diff, 0.0)), 0.0)
        att = jnp.einsum('nhtsd,nhsd->nhts', qc[:, :, :, None, :] * decay, kc)
        o = jnp.einsum('nhts,nhsv->nhtv', att, vc) + jnp.einsum('nhtd,nhdv->nhtv', qc * jnp.exp(b), s)
        b_last = b[:, :, -1:, :]
        s_new = jnp.exp(b_last[:, :, 0, :])[..., None] * s + jnp.einsum('nhsd,nhsv->nhdv', kc * jnp.exp(b_last - b), vc)
        return s_new, o

    s_fin, o = lax.scan(step, s0, (to_chunks(q), to_chunks(k), to_chunks(v), to_chunks(logf)))
    o = o.transpose(1, 0, 3, 2, 4).reshape(n, nc * c, HG_HEADS, HG_DV)[:, :l]
    return o, s_fin

def hgrn2_mixer(x, s0, w_in, lb, gnorm, w_out):
    f32 = jnp.float32
    n, l, _ = x.shape
    q, fz, vi, g = jnp.split(x @ w_in, [HG_F, 2 * HG_F, 2 * HG_F + D_MODEL], axis=-1)
    q = jax.nn.silu(q.astype(f32)).reshape(n, l, HG_HEADS, HG_DK)
    fz = fz.astype(f32).reshape(n, l, HG_HEADS, HG_DK)
    lb = lb.astype(f32).reshape(HG_HEADS, HG_DK)
    f = lb + (1.0 - lb) * jax.nn.sigmoid(fz)
    logf = jnp.log(f)
    k = (1.0 - lb) * jax.nn.sigmoid(-fz)
    v = vi.astype(f32).reshape(n, l, HG_HEADS, HG_DV)
    o, s_fin = hgrn2_chunk_scan(q, k, v, logf, s0.astype(f32))
    o = o * lax.rsqrt(jnp.mean(jnp.square(o), -1, keepdims=True) + RMS_EPS) * gnorm.astype(f32).reshape(HG_HEADS, HG_DV)
    o = o.reshape(n, l, D_MODEL) * jax.nn.silu(g.astype(f32))
    return o.astype(x.dtype) @ w_out, s_fin

def t5_bucket(rel):
    n = jnp.maximum(rel, 0)
    exact = REL_BUCKETS // 2
    nf = jnp.maximum(n, exact).astype(jnp.float32)
    large = exact + (jnp.log(nf / exact) / math.log(REL_MAX_DIST / exact) * (REL_BUCKETS - exact)).astype(jnp.int32)
    large = jnp.minimum(large, REL_BUCKETS - 1)
    return jnp.where(n < exact, n, large)

def dsa_project(x, w_in, kln_g, kln_b):
    n, l, _ = x.shape
    hd = AT_HEADS * AT_DH
    qd = IDX_HEADS * IDX_DIM
    q, k, v, qi, ki, wi = jnp.split(x @ w_in, [hd, 2 * hd, 3 * hd, 3 * hd + qd, 3 * hd + qd + IDX_DIM], axis=-1)
    q = q.reshape(n, l, AT_HEADS, AT_DH)
    k = k.reshape(n, l, AT_HEADS, AT_DH)
    v = v.reshape(n, l, AT_HEADS, AT_DH)
    qi = qi.reshape(n, l, IDX_HEADS, IDX_DIM) * (IDX_DIM ** -0.5)
    ki = layer_norm(ki, kln_g, kln_b)
    wi = wi * (IDX_HEADS ** -0.5)
    return q, k, v, qi, ki, wi

def dsa_attend(q, qi, wi, qpos, kidx, gather_kv, rel_bias, n_sel):
    l = kidx.shape[0]
    dots = jax.nn.relu(jnp.einsum('qhd,sd->qhs', qi, kidx).astype(jnp.float32))
    score = jnp.einsum('qh,qhs->qs', wi.astype(jnp.float32), dots)
    kpos = jnp.arange(l, dtype=jnp.int32)
    admissible = kpos[None, :] <= qpos[:, None]
    _, sel = lax.top_k(jnp.where(admissible, score, NEG_BIG), n_sel)
    valid = sel <= qpos[:, None]
    k_sel, v_sel = gather_kv(sel)
    bias = rel_bias[t5_bucket(qpos[:, None] - sel)].astype(jnp.float32)
    logits = jnp.einsum('qhd,qkhd->qhk', q, k_sel).astype(jnp.float32) * (AT_DH ** -0.5) + bias.transpose(0, 2, 1)
    logits = jnp.where(valid[:, None, :], logits, NEG_BIG)
    p = jax.nn.softmax(logits, axis=-1)
    return jnp.einsum('qhk,qkhd->qhd', p.astype(v_sel.dtype), v_sel)

def dsa_prompt(x, w_in, kln_g, kln_b, w_out, rel_bias):
    n, l, _ = x.shape
    q, k, v, qi, ki, wi = dsa_project(x, w_in, kln_g, kln_b)
    nb = l // Q_BLOCK
    n_sel = min(TOPK_MAX, l // 4)

    def blockify(a):
        return a.reshape((n * nb, Q_BLOCK) + a.shape[2:])

    b_ids = jnp.repeat(jnp.arange(n, dtype=jnp.int32), nb)
    blk_ids = jnp.tile(jnp.arange(nb, dtype=jnp.int32), n)

    def one_block(args):
        b, blk, qb, qib, wib = args
        qpos = blk * Q_BLOCK + jnp.arange(Q_BLOCK, dtype=jnp.int32)
        gather = lambda sel: (k[b, sel], v[b, sel])
        return dsa_attend(qb, qib, wib, qpos, ki[b], gather, rel_bias, n_sel)

    o = lax.map(one_block, (b_ids, blk_ids, blockify(q), blockify(qi), blockify(wi)))
    return o.reshape(n, l, AT_HEADS * AT_DH) @ w_out, k, v, ki

def dsa_sample(x, j, cache_k, cache_v, cache_kidx, page_table, w_in, kln_g, kln_b, w_out, rel_bias):
    n, l, _ = x.shape
    past = page_table.shape[1] * PAGE_SIZE
    n_sel = min(TOPK_MAX, (past + l) // 4)
    q, k, v, qi, ki, wi = dsa_project(x, w_in, kln_g, kln_b)
    qpos = past + jnp.arange(l, dtype=jnp.int32)

    def one_seq(qs, qis, wis, ks, vs, kis, pt):
        kidx_past = cache_kidx[j, pt].reshape(past, IDX_DIM)
        kidx_all = jnp.concatenate([kidx_past, kis], axis=0)

        def gather(sel):
            in_past = sel < past
            sp = jnp.minimum(sel, past - 1)
            phys = pt[sp // PAGE_SIZE]
            off = sp % PAGE_SIZE
            sn = jnp.clip(sel - past, 0, l - 1)
            m = in_past[..., None, None]
            return (jnp.where(m, cache_k[j, phys, off], ks[sn]), jnp.where(m, cache_v[j, phys, off], vs[sn]))

        return dsa_attend(qs, qis, wis, qpos, kidx_all, gather, rel_bias, n_sel)

    o = jax.vmap(one_seq)(q, qi, wi, k, v, ki, page_table)
    return o.reshape(n, l, AT_HEADS * AT_DH) @ w_out, k, v, ki

def s5_mixer(x, h0_re, h0_im, a_re, a_im, log_dt, b_re, b_im, c_re, c_im, d_skip, w_glu, b_glu):
    f32 = jnp.float32
    n, l, _ = x.shape
    u = x.astype(f32).reshape(n, l, S5_GROUPS, S5_GROUP)
    dt = jnp.exp(log_dt.astype(f32))[:, None]
    ar, ai = a_re.astype(f32), a_im.astype(f32)
    mag = jnp.exp(dt * ar)
    abar_re, abar_im = mag * jnp.cos(dt * ai), mag * jnp.sin(dt * ai)
    den = ar * ar + ai * ai
    nr, ni = abar_re - 1.0, abar_im
    z_re = (nr * ar + ni * ai) / den
    z_im = (ni * ar - nr * ai) / den
    br, bi = b_re.astype(f32), b_im.astype(f32)
    bbar_re = z_re[..., None] * br - z_im[..., None] * bi
    bbar_im = z_re[..., None] * bi + z_im[..., None] * br
    bu_re = jnp.einsum('nlgk,gpk->nlgp', u, bbar_re)
    bu_im = jnp.einsum('nlgk,gpk->nlgp', u, bbar_im)
    h0r, h0i = h0_re.astype(f32), h0_im.astype(f32)
    bu_re = bu_re.at[:, 0].add(abar_re * h0r - abar_im * h0i)
    bu_im = bu_im.at[:, 0].add(abar_re * h0i + abar_im * h0r)
    a_l_re = jnp.broadcast_to(abar_re, bu_re.shape)
    a_l_im = jnp.broadcast_to(abar_im, bu_im.shape)

    def combine(e1, e2):
        a1r, a1i, b1r, b1i = e1
        a2r, a2i, b2r, b2i = e2
        return (a2r * a1r - a2i * a1i, a2r * a1i + a2i * a1r,
                a2r * b1r - a2i * b1i + b2r, a2r * b1i + a2i * b1r + b2i)

    _, _, hr, hi = lax.associative_scan(combine, (a_l_re, a_l_im, bu_re, bu_im), axis=1)
    y = jnp.einsum('nlgp,gkp->nlgk', hr, c_re.astype(f32)) - jnp.einsum('nlgp,gkp->nlgk', hi, c_im.astype(f32))
    y = y.reshape(n, l, D_MODEL) + d_skip.astype(f32) * x.astype(f32)
    g = jax.nn.gelu(y).astype(x.dtype)
    val, gate = jnp.split(g @ w_glu + b_glu, 2, axis=-1)
    out = val * jax.nn.sigmoid(gate.astype(f32))
    return out.astype(x.dtype), hr[:, -1], hi[:, -1]

def setup_inputs(seed: int = 0) -> dict:
    key = jax.random.key(seed)
    ks = iter(jax.random.split(key, 48))
    f32 = jnp.float32
    nrm = lambda shape, s: jax.random.normal(next(ks), shape, f32) * s
    n_pages = PAST_LEN // PAGE_SIZE
    n_used = DEC_BATCH * n_pages
    n_pool = n_used + max(1, n_used // 4)
    page_table = jax.random.permutation(next(ks), n_pool)[:n_used].reshape(DEC_BATCH, n_pages).astype(jnp.int32)
    a_im0 = jnp.pi * jnp.arange(S5_STATE, dtype=f32)
    w_glu = nrm((N_C, D_MODEL, 2 * D_MODEL), D_MODEL ** -0.5)
    w_glu = w_glu * jnp.concatenate([jnp.full((D_MODEL,), DN_BETA, f32), jnp.ones((D_MODEL,), f32)])
    return {
        'x_prompt': nrm((BATCH, SEQ, D_MODEL), 1.0),
        'x_sample': nrm((DEC_BATCH, DEC_SEQ, D_MODEL), 1.0),
        'state_hgrn': nrm((N_A, DEC_BATCH, HG_HEADS, HG_DK, HG_DV), 0.3),
        'cache_k': nrm((N_B, n_pool, PAGE_SIZE, AT_HEADS, AT_DH), 1.0),
        'cache_v': nrm((N_B, n_pool, PAGE_SIZE, AT_HEADS, AT_DH), 1.0),
        'cache_kidx': nrm((N_B, n_pool, PAGE_SIZE, IDX_DIM), 1.0),
        'page_table': page_table,
        'state_s5_re': nrm((N_C, DEC_BATCH, S5_GROUPS, S5_STATE), 0.1),
        'state_s5_im': nrm((N_C, DEC_BATCH, S5_GROUPS, S5_STATE), 0.1),
        'hg_w_in': nrm((N_A, D_MODEL, HG_IN), D_MODEL ** -0.5),
        'hg_lb': nrm((DEPTH, HG_F), 0.1),
        'hg_gnorm': 1.0 + nrm((N_A, D_MODEL), 0.05),
        'hg_w_out': nrm((N_A, D_MODEL, D_MODEL), D_MODEL ** -0.5 * DN_BETA),
        'dsa_w_in': nrm((N_B, D_MODEL, DSA_IN), D_MODEL ** -0.5),
        'dsa_kln_g': 1.0 + nrm((N_B, IDX_DIM), 0.05),
        'dsa_kln_b': nrm((N_B, IDX_DIM), 0.02),
        'dsa_w_out': nrm((N_B, AT_HEADS * AT_DH, D_MODEL), (AT_HEADS * AT_DH) ** -0.5 * DN_BETA),
        'rel_bias': nrm((REL_BUCKETS, AT_HEADS), 0.5),
        's5_a_re': -0.5 + nrm((N_C, S5_GROUPS, S5_STATE), 0.01),
        's5_a_im': a_im0 + nrm((N_C, S5_GROUPS, S5_STATE), 0.01),
        's5_log_dt': jax.random.uniform(next(ks), (N_C, S5_GROUPS), f32, math.log(S5_DT_MIN), math.log(S5_DT_MAX)),
        's5_b_re': nrm((N_C, S5_GROUPS, S5_STATE, S5_GROUP), (2 * S5_GROUP) ** -0.5),
        's5_b_im': nrm((N_C, S5_GROUPS, S5_STATE, S5_GROUP), (2 * S5_GROUP) ** -0.5),
        's5_c_re': nrm((N_C, S5_GROUPS, S5_GROUP, S5_STATE), (2 * S5_STATE) ** -0.5),
        's5_c_im': nrm((N_C, S5_GROUPS, S5_GROUP, S5_STATE), (2 * S5_STATE) ** -0.5),
        's5_d': nrm((N_C, D_MODEL), 1.0),
        's5_w_glu': w_glu,
        's5_b_glu': nrm((N_C, 2 * D_MODEL), 0.02),
        'ln_mix_g': 1.0 + nrm((DEPTH, D_MODEL), 0.05),
        'ln_mix_b': nrm((DEPTH, D_MODEL), 0.02),
        'mlp_w1': nrm((DEPTH, D_MODEL, FFN_HIDDEN), D_MODEL ** -0.5),
        'mlp_w2': nrm((DEPTH, FFN_HIDDEN, D_MODEL), FFN_HIDDEN ** -0.5 * DN_BETA),
        'ln_ffn_g': 1.0 + nrm((DEPTH, D_MODEL), 0.05),
        'ln_ffn_b': nrm((DEPTH, D_MODEL), 0.02),
    }

def reference(x_prompt, x_sample, state_hgrn, cache_k, cache_v, cache_kidx, page_table, state_s5_re, state_s5_im,
              hg_w_in, hg_lb, hg_gnorm, hg_w_out, dsa_w_in, dsa_kln_g, dsa_kln_b, dsa_w_out, rel_bias,
              s5_a_re, s5_a_im, s5_log_dt, s5_b_re, s5_b_im, s5_c_re, s5_c_im, s5_d, s5_w_glu, s5_b_glu,
              ln_mix_g, ln_mix_b, mlp_w1, mlp_w2, ln_ffn_g, ln_ffn_b):
    f32 = jnp.float32
    lb_sm = jax.nn.softmax(hg_lb.astype(f32), axis=0)
    lower_bounds = jnp.cumsum(lb_sm, axis=0) - lb_sm[0]
    xp, xs = x_prompt, x_sample
    n_p = xp.shape[0]
    hg_p, hg_s = [], []
    k_p, v_p, ki_p, k_s, v_s, ki_s = [], [], [], [], [], []
    s5r_p, s5i_p, s5r_s, s5i_s = [], [], [], []
    for i in range(DEPTH):
        j = i // N_MIXERS
        kind = i % N_MIXERS
        if kind == 0:
            zero = jnp.zeros((n_p, HG_HEADS, HG_DK, HG_DV), f32)
            mp, st_p = hgrn2_mixer(xp, zero, hg_w_in[j], lower_bounds[i], hg_gnorm[j], hg_w_out[j])
            ms, st_s = hgrn2_mixer(xs, state_hgrn[j], hg_w_in[j], lower_bounds[i], hg_gnorm[j], hg_w_out[j])
            hg_p.append(st_p)
            hg_s.append(st_s)
        elif kind == 1:
            mp, kk, vv, kki = dsa_prompt(xp, dsa_w_in[j], dsa_kln_g[j], dsa_kln_b[j], dsa_w_out[j], rel_bias)
            ms, kk2, vv2, kki2 = dsa_sample(xs, j, cache_k, cache_v, cache_kidx, page_table,
                                           dsa_w_in[j], dsa_kln_g[j], dsa_kln_b[j], dsa_w_out[j], rel_bias)
            k_p.append(kk)
            v_p.append(vv)
            ki_p.append(kki)
            k_s.append(kk2)
            v_s.append(vv2)
            ki_s.append(kki2)
        else:
            zr = jnp.zeros((n_p, S5_GROUPS, S5_STATE), f32)
            s5w = (s5_a_re[j], s5_a_im[j], s5_log_dt[j], s5_b_re[j], s5_b_im[j], s5_c_re[j], s5_c_im[j],
                   s5_d[j], s5_w_glu[j], s5_b_glu[j])
            mp, hr, hi = s5_mixer(xp, zr, zr, *s5w)
            ms, hr2, hi2 = s5_mixer(xs, state_s5_re[j], state_s5_im[j], *s5w)
            s5r_p.append(hr)
            s5i_p.append(hi)
            s5r_s.append(hr2)
            s5i_s.append(hi2)
        xp = layer_norm(DN_ALPHA * xp + mp, ln_mix_g[i], ln_mix_b[i])
        xs = layer_norm(DN_ALPHA * xs + ms, ln_mix_g[i], ln_mix_b[i])
        xp = layer_norm(DN_ALPHA * xp + sq_relu_mlp(xp, mlp_w1[i], mlp_w2[i]), ln_ffn_g[i], ln_ffn_b[i])
        xs = layer_norm(DN_ALPHA * xs + sq_relu_mlp(xs, mlp_w1[i], mlp_w2[i]), ln_ffn_g[i], ln_ffn_b[i])
    return (xp, xs, jnp.stack(hg_p), jnp.stack(hg_s), jnp.stack(k_p), jnp.stack(v_p), jnp.stack(ki_p),
            jnp.stack(k_s), jnp.stack(v_s), jnp.stack(ki_s), jnp.stack(s5r_p), jnp.stack(s5i_p),
            jnp.stack(s5r_s), jnp.stack(s5i_s))


_drawn_inputs = setup_inputs


def setup_inputs(seed=0):
    import zlib

    import numpy as np

    out = dict(_drawn_inputs(seed))
    spreads = {}
    factors = {'hg_gnorm': 4.723, 's5_a_re': 4.326, 's5_c_re': 8.0, 's5_c_im': 8.0, 's5_b_glu': 6.887}
    for name, (base, spread) in spreads.items():
        noise = np.random.default_rng([zlib.crc32(name.encode()), seed]).standard_normal(out[name].shape)
        drawn = base * np.exp(spread * noise) if base else spread * noise
        out[name] = __import__('jax').numpy.asarray(drawn.astype(out[name].dtype))
    for name, factor in factors.items():
        out[name] = (out[name] * factor).astype(out[name].dtype)
    return out
```

```python
import math
from contextlib import ExitStack

import numpy as np
import concourse.bass as bass
from concourse import mybir

F32 = mybir.dt.float32
F32R = mybir.dt.float32r
I32 = mybir.dt.int32
U8 = mybir.dt.uint8
ALU = mybir.AluOpType
ACT = mybir.ActivationFunctionType
AX = mybir.AxisListType

P = 128
D = 1024
KT = D // P
NP_ = 512
NS = 8
N = NP_ + NS
NH2 = N // 2
TB = NP_ // P
DEPTH = 4
KINDS = [i % 3 for i in range(DEPTH)]
HID = 4 * D
HHALF = HID // 2 // P
HEADS = 8
ALPHA = (2 * DEPTH) ** 0.25
LN_EPS = 1e-5
RMS_EPS = 1e-6
DH = 128
IH = 8
IDX_DIM = 64
PAST = 256
SK = PAST + 1
HN = HEADS * NS
PSEL = 128
SSEL = SK // 4
REL = 32
ROW = 640
NPOOL = 20
NEG = -1e30
TAKEN = -3e38
LEVELS = 7
RAW = 2
SPL = 4
AHEAD = SPL - 1

S5T = 32
FINE = 32
ANG = 9
ROUND = 1.5 * 2 ** 23
TURN_HI = 6.28125
TURN_LO = 2 * math.pi - TURN_HI
PI32 = 3.14159250259

MIX_CHUNKS = [40, 37, 16]
MLP_CHUNKS = 64
MLP_TILES = 2 * (HHALF + KT)


class Chain:

    def __init__(self, eng, sem):
        self.eng, self.sem, self.n, self.at = eng, sem, 0, None

    def mark(self, ins):
        ins.then_inc(self.sem, 1)
        self.n += 1

    def wait(self):
        self.eng.wait_ge(self.sem, self.n if self.at is None else self.at + self.n)

    def step(self, ins):
        self.mark(ins)
        self.wait()

    def loop(self, i, per):
        self.at, self.per, self.n0 = i * per, per, self.n

    def end(self, times):
        assert self.n - self.n0 == self.per, (self.n, self.n0, self.per)
        self.at, self.n = None, self.n0 + self.per * times


def halves(ap):
    return ap.rearrange("p (h n) -> p h n", h=2)


def trunk(nc, I, O, kinds=KINDS):
    ctx = ExitStack()

    def sb(name, shape, dt=F32, c=ctx):
        return c.enter_context(nc.sbuf_tensor(name, shape, dt))

    def sem(name):
        return ctx.enter_context(nc.semaphore(name))

    x = sb("x", [P, KT, N])
    xh = sb("xh", [P, KT, N], F32R)
    xl = sb("xl", [P, KT, N], F32R)
    raw = sb("raw", [P, RAW, KT * P])
    wh = sb("wh", [P, SPL, KT * P], F32R)
    wl = sb("wl", [P, SPL, KT * P], F32R)
    r = sb("r", [P, KT, N])
    lw = sb("lw", [P, 8, N])
    rsum, rsq, mean, rstd = lw[:, 0, :], lw[:, 1, :], lw[:, 4, :], lw[:, 5, :]
    ident = sb("ident", [P, P])
    ones_mean = sb("ones_mean", [P, P])
    ones_head = sb("ones_head", [P, P])
    lnp = sb("lnp", [P, 4, DEPTH, KT])
    keep = sb("keep", [P, NP_])
    eps = sb("eps", [P, 2])
    hgp = sb("hgp", [P, 2, KT])
    lbp = sb("lbp", [P, DEPTH, KT])
    lb = sb("lb", [P, 2, 2, KT])
    lbt = sb("lbt", [P, 3, KT])
    kiln = sb("kiln", [P, 2])
    ones = sb("ones", [P, P])
    ones_idx = sb("ones_idx", [P, P])
    cmask = sb("cmask", [P, P])
    pts = sb("pts", [1, 2 * NS], I32)

    c = ExitStack()
    hh = sb("hh", [P, HHALF, N], F32R, c)
    hl = sb("hl", [P, HHALF, N], F32R, c)
    c.close()
    c = ExitStack()
    mixA = sb("mixA", [P, KT, N], F32, c)
    qt = sb("qt", [P, LEVELS, NP_ // 2], F32, c)
    kt = sb("kt", [P, LEVELS, NP_], F32, c)
    dd = sb("dd", [P, 2, NP_], F32, c)
    ee = sb("ee", [P, 2, NP_], F32, c)
    kp = sb("kp", [P, NP_], F32, c)
    ktok = sb("ktok", [P, NP_], F32, c)
    vtok = sb("vtok", [P, NP_], F32, c)
    att = sb("att", [P, NP_], F32, c)
    st = sb("st", [P, 5, P], F32, c)
    s0b = sb("s0", [P, 2, NS, P], F32, c)
    vz = sb("vz", [NS, NS, P], F32, c)
    tok8 = sb("tok8", [NS, 2, P], F32, c)
    lmask = sb("lmask", [P, LEVELS, NP_ // 2], U8, c)
    qe = sb("qe", [P, NP_], F32, c)
    c.close()
    c = ExitStack()
    mixB = sb("mixB", [P, KT, N], F32, c)
    vtk = sb("vtk", [P, TB, HEADS, P], F32, c)
    qi = sb("qi", [P, 4, N], F32, c)
    sc = sb("sc", [P, TB, NP_], F32, c)
    pg = sb("pg", [P, 2, 2, D], F32, c)
    bsm = sb("bsm", [P, 12, SK + 3], F32, c)
    relb = sb("relb", [REL, HEADS + HN], F32, c)
    oh_p = sb("oh_p", [REL, ROW + SK], F32, c)
    c.close()
    c = ExitStack()
    mixC = sb("mixC", [P, KT, N], F32, c)
    bbar = sb("bbar", [P, 2, KT, P], F32, c)
    ph = sb("ph", [P, 2, 4, NP_], F32, c)
    rot = sb("rot", [P, 2, 2, NP_], F32, c)
    fine = sb("fine", [P, 2, S5T, FINE], F32, c)
    middle = sb("middle", [P, 2, S5T, 4], F32, c)
    top = sb("top", [P, 2, S5T, 4], F32, c)
    spun = sb("spun", [P, 4, 3, P], F32, c)
    s5v = sb("s5v", [P, 14, S5T], F32, c)
    ang = sb("ang", [P, 4, ANG, S5T], F32, c)
    s5s = sb("s5s", [P, 2, S5T, NS], F32, c)
    s5h = sb("s5h", [P, 2, S5T, NS], F32, c)
    x4 = sb("x4", [P, KT, 4, NS], F32, c)
    stmp = sb("stmp", [P, 4, S5T * NS], F32, c)
    s5f = sb("s5f", [P, 2, S5T], F32, c)
    s5d = sb("s5d", [P, KT], F32, c)
    s5g = sb("s5g", [P, 2 * KT], F32, c)
    c.close()
    lwf, rf = (a[:].rearrange("p a n -> p (a n)") for a in (lw, r))
    braw = lwf[:, 0:2 * D].rearrange("p (a k d) -> p a k d", a=2, d=P)
    bprod = lwf[:, 2 * D:4 * D].rearrange("p (a k d) -> p a k d", a=2, d=P)
    zx = lwf[:, 2 * D:4 * D].rearrange("p (a t f) -> p a t f", a=2, f=32)
    turned = lwf[:, 0:4 * NP_].rearrange("p (a t) -> p a t", a=4)
    uin = lwf[:, 4 * NP_:6 * NP_].rearrange("p (a t) -> p a t", a=2)
    gst = lwf[:, 6 * NP_:8 * NP_].rearrange("p (a t) -> p a t", a=2)
    cmat = rf[:, 0:3 * D].rearrange("p (a t k) -> p a t k", a=3, k=32)
    rtmp = rf[:, 3 * D:4 * D].rearrange("p (a t) -> p a t", a=2)
    kT = r
    vT = lw[:, 0:2, :]
    kiT = lw[:, 2, :]
    tb = lw[:, 0:2, 0:NP_]
    rl = lw[:, 3:5, :]
    pb_ = lw[:, 3:5, :]
    pt_ = lw[:, 5:7, :]
    fq = r
    gt = lw[:, 0:2, :]
    sgn = lw[:, 2, :]
    ot = lw[:, 3, :]
    osq = lw[:, 4, :]
    orstd = lw[:, 5, :]
    lf = lw[:, 6, :]
    bb = lw[:, 7, :]

    lp = ctx.enter_context(nc.psum_tensor("lp", [P, 4, 512], F32))
    mb = ctx.enter_context(nc.psum_tensor("mb", [P, 4, 512], F32))

    raw_loaded = [sem(f"raw_loaded{i}") for i in range(RAW)]
    w_high, w_low, chunk_done = sem("w_high"), sem("w_low"), sem("chunk_done")
    tile_out = sem("tile_out")
    h_ready = sem("h_ready")
    sq_ready, sq_added = sem("sq_ready"), sem("sq_added")
    sum_ready, stats_ready, var_ready, rstd_ready = sem("sum_ready"), sem("stats_ready"), sem("var_ready"), sem("rstd_ready")
    norm_ready, x_ready, xh_ready, xl_ready = sem("norm_ready"), sem("x_ready"), sem("xh_ready"), sem("xl_ready")
    x_loaded = [sem(f"x_loaded{i}") for i in range(4)]
    const_loaded, masks_loaded, consts_set, lb_ready = (
        sem("const_loaded"), sem("masks_loaded"), sem("consts_set"), sem("lb_ready"))
    dve_link, act_link, pool_link = sem("dve_link"), sem("act_link"), sem("pool_link")
    stored = sem("stored")
    zeroed = sem("zeroed")
    mix_ready = sem("mix_ready")
    gates, sig_ready, f_ready, lf_ready, b_ready, eb_ready = (sem("gates"), sem("sig_ready"), sem("f_ready"),
                                                            sem("lf_ready"), sem("b_ready"), sem("eb_ready"))
    d_ready, e_ready, kp_ready, kt_ready, qt_ready = (sem("d_ready"), sem("e_ready"), sem("kp_ready"), sem("kt_ready"),
                                                     sem("qt_ready"))
    tok_ready, tok_copied, att_ready, att_merged = sem("tok_ready"), sem("tok_copied"), sem("att_ready"), sem("att_merged")
    upd_ready, states_ready, vz_ready, su_ready = sem("upd_ready"), sem("states_ready"), sem("vz_ready"), sem("su_ready")
    sf_ready, snew_ready, o_ready, so_ready = sem("sf_ready"), sem("snew_ready"), sem("o_ready"), sem("so_ready")
    osq_ready, ms_ready, orstd_ready = sem("osq_ready"), sem("ms_ready"), sem("orstd_ready")
    s0_loaded, s0_stored = ([sem(f"s0_{a}{b}") for b in range(2)] for a in ("loaded", "stored"))
    st_stored = sem("st_stored")

    (ki_raw, ki_stats, ki_var, ki_rstd, ki_norm, ki_ready, wi_psum, wi_ready, w3_ready, dot_ready, relu_done, score_added,
     kx_own, sdot_ready, srelu_done, s8_ready, s8_out, top_done, sneg_ready, b_loaded, rows_ready, rows_out, rows_stored,
     vtr_ready, vtr_out, pages_used, spsum, slog, sy_ready, sprod, sz_ready, sz_out, sl_ready, sexp, sp_ready, spt_ready,
     spt_out, sbc_out, log_ready, l_ready, exp_done, p_ready, ptr_ready, ptr_out, pv_ready, pv_out) = (
        sem("b_" + n) for n in
        """ki_raw ki_stats ki_var ki_rstd ki_norm ki_ready wi_psum wi_ready w3_ready dot_ready relu_done score_added
     kx_own sdot_ready srelu_done s8_ready s8_out top_done sneg_ready loaded rows_ready rows_out rows_stored
     vtr_ready vtr_out pages_used spsum slog sy_ready sprod sz_ready sz_out sl_ready sexp sp_ready spt_ready
     spt_out sbc_out log_ready l_ready exp_done p_ready ptr_ready ptr_out pv_ready pv_out""".split())
    kx_loaded = [sem("b_kx_loaded0"), sem("b_kx_loaded1")]
    pg_loaded = [sem("b_pg_loaded0"), sem("b_pg_loaded1")]
    tb_loaded = [sem("b_tb_loaded0"), sem("b_tb_loaded1")]
    v_stored = [sem("b_v_stored0"), sem("b_v_stored1")]
    pt_loaded, kv_stored = sem("b_pt_loaded"), sem("b_kv_stored")
    x4_ready, first_ready, spun_ready, rot_ready = (sem("s5_" + n) for n in ("x4_ready", "first_ready", "spun_ready", "rot_ready"))
    (s5_loaded, s5_dt, s5_arg, s5_mag, s5_red, s5_sin, z_ready, z_psum, bbar_ready, sbu_ready, s5h_ready, c_ready,
     syc_ready, bu_ready, turned_ready, u_ready, g_ready, ph_dve, ph_pool, fin_ready, y_done, gin_ready, glu_done,
     s5_stored) = (
        sem("s5_" + n) for n in
        """loaded dt arg mag red sin z_ready z_psum bbar_ready sbu_ready h_ready c_ready
     syc_ready bu_ready turned_ready u_ready g_ready ph_dve ph_pool fin_ready y_done gin_ready glu_done
     stored""".split())
    bias_rows = nc.dram_tensor("bias_rows", (HEADS, P, ROW), F32, kind="Internal").ap()
    kx = bsm[:, 0:2, 0:SK]
    srl = bsm[0:4, 2:4, 0:SK]
    s8 = bsm[0:NS, 4, 0:SK]
    zb = bsm[0:HN, 5, 0:SK]
    sl = bsm[0:HN, 6, 0:SK]
    w3 = bsm[0:4, 7, 0:2 * NS * NS].rearrange("k (a n m) -> k a n m", a=2, n=NS)
    wi8 = bsm[0:4, 8, 0:2 * NS]
    ltok = bsm[:, 9, 0:P]
    sprodt = bsm[:, 9, P:P + HN]
    sptt = bsm[:, 10, 0:P]
    sdiag = bsm[0:HN, 10, P:P + HN]
    sbc = bsm[:, 11, 0:HN]
    rep8 = bsm[0:NS, 7, P:P + HN]
    oh4 = bsm[0:4, 7, P + HN:P + 2 * HN]
    vs8 = bsm[:, 8, 16:80].rearrange("p (h n) -> p h n", h=HEADS)
    wtk = bsm[:, 8, 80:112].rearrange("p (b h) -> p b h", h=IH)
    top8 = bsm[:, 8, 112:120]
    wwi = bsm[:, 8, 128:192].rearrange("p (k h) -> p k h", h=IH)
    s_small = bsm[:, 11, HN:HN + 8]
    a_small = bsm[:, 11, HN + 8:HN + 24]

    rowb = bsm[0:HEADS, 9:12, :].rearrange("p a b -> p (a b)")[:, 0:ROW]

    def nmx(u):
        return a_small[:, 4 + u % 2:5 + u % 2]

    def sme(u):
        return a_small[:, 8 + u % 2:9 + u % 2]

    UNITS = [(h, qb) for h in range(HEADS) for qb in range(TB)]
    IUNITS = [(qb, h) for qb in range(1, TB) for h in range(IH)]

    plan, cn, tn, occ, mixes = [], 0, 0, [0, 0, 0], 0
    for i, kind in enumerate(kinds):
        plan.append(dict(kind=kind, c=cn, t=tn, cm=cn + MIX_CHUNKS[kind], tm=tn + MIX_CHUNKS[kind], i=i, j=occ[kind],
                         mix=mixes))
        mixes += 1 if kind == 1 else 8
        occ[kind] += 1
        cn += MIX_CHUNKS[kind] + MLP_CHUNKS
        tn += MIX_CHUNKS[kind] + MLP_TILES
    CHUNKS = cn
    L = len(kinds)

    block = ctx.enter_context(nc.Block())

    @block.sync
    def _(sp):
        def load(n, s):
            sp.dma_start(raw[:, s, :], I["wstream"][bass.ds(n, 1), :, :].rearrange("o p w -> (o p) w")
                         ).then_inc(raw_loaded[s], 16)

        for n in range(RAW):
            load(n, n % RAW)
        groups = (CHUNKS - RAW) // 4
        with sp.Fori(0, groups) as i:
            for c in range(4):
                n = RAW + c
                sp.wait_ge(w_low, i * 4 + (n - RAW + 1))
                load(i * 4 + n, n % RAW)
        for n in range(RAW + 4 * groups, CHUNKS):
            sp.wait_ge(w_low, n - RAW + 1)
            load(n, n % RAW)

        for k in range(4):
            sp.wait_ge(x_ready, 16 * L - 8 + 2 * k + 2)
            sp.dma_start(O["yT"][:, 2 * k:2 * k + 2, :], x[:, 2 * k:2 * k + 2, :]).then_inc(stored, 16)
        sp.wait_ge(stored, 64)

    @block.gpsimd
    def _(pool):
        link = Chain(pool, pool_link)

        def low(n, s, r_):
            pool.wait_ge(w_high, n + 1)
            pool.tensor_tensor(wl[:, s, :], raw[:, r_, :], wh[:, s, :].bitcast(F32), ALU.subtract).then_inc(w_low, 1)

        def low_at(n):
            if n < CHUNKS:
                low(n, n % SPL, n % RAW)

        def split(src, n0, ms=range(KT)):
            for m in ms:
                pool.wait_ge(xh_ready, n0 + m + 1)
                pool.tensor_tensor(xl[:, m, :], src[:, m, :], xh[:, m, :].bitcast(F32), ALU.subtract
                                   ).then_inc(xl_ready, 1)

        def square_sum(ln, m):
            if m < KT - 1:
                pool.wait_ge(sq_ready, 8 * ln + m + 1)
                pool.wait_ge(sq_added, 7 * ln + m)
                pool.tensor_tensor(rsq, rsq, lw[:, 2 + m % 2, :], ALU.add).then_inc(sq_added, 1)

        def clear_sums(ln):
            if ln:
                pool.wait_ge(stats_ready, ln)
            pool.memset(rsq, 0.0).then_inc(zeroed, 1)
            pool.wait_ge(zeroed, ln + 1)

        pool.memset(ones_mean[:], 1.0 / D).then_inc(consts_set, 1)
        pool.memset(ones_head[:], 1.0 / P).then_inc(consts_set, 1)
        pool.memset(eps[:, 0:1], LN_EPS).then_inc(consts_set, 1)
        pool.memset(eps[:, 1:2], RMS_EPS).then_inc(consts_set, 1)
        pool.memset(keep[:], 1.0).then_inc(consts_set, 1)
        pool.memset(ones[:], 1.0).then_inc(consts_set, 1)
        pool.wait_ge(consts_set, 6)
        pool.memset(keep[:, 0:NP_:P], 0.0).then_inc(consts_set, 1)
        for n in range(AHEAD):
            low_at(n)
        for k in range(4):
            pool.wait_ge(x_loaded[k], 16)
            split(x, 0, (2 * k, 2 * k + 1))

        for y in plan:
            ln = 2 * y["i"]
            if y["kind"] == 0:
                g0 = 8 * y["j"]
                for h in range(HEADS + 1):
                    def ahead(j):
                        if h < HEADS:
                            low_at(y["c"] + 4 * h + j + AHEAD)

                    ahead(0)
                    if h:
                        G, p = g0 + h - 1, (h - 1) % 2
                        pool.wait_ge(f_ready, 2 * (G + 1))
                        pool.wait_ge(e_ready, 8 * G + 1)
                        if G:
                            pool.wait_ge(tok_ready, G)
                        pool.tensor_tensor(kp[:], fq[:, 4 * p + 1, 0:NP_], ee[:, 0, :], ALU.mult).then_inc(kp_ready, 1)
                        ahead(1)
                        pool.wait_ge(s0_loaded[G % 2], 16 * (G // 2 + 1))
                        fs = fq[:, 4 * p, NP_:N].unsqueeze(2).to_broadcast([P, NS, P])
                        pool.tensor_tensor(s0b[:, G % 2], s0b[:, G % 2], fs, ALU.mult).then_inc(sf_ready, 1)
                    else:
                        ahead(1)
                    ahead(2)
                    ahead(3)
                split(mixA, 8 * (3 * y["i"] + 1))
                tail = y["c"] + 32
            if y["kind"] == 1:
                regs = {}

                def page(slot_ap, src, k, done):
                    pid = pool.value_load(pts[0:1, k:k + 1], min_val=0, max_val=NPOOL - 1)
                    pool.dma_start(slot_ap, src[bass.ds(pid, 1), :, :].rearrange("o p w -> (o p) w")).then_inc(done, 16)

                def index_pages(n):
                    if n >= 2:
                        pool.wait_ge(sdot_ready, n - 1)
                    for g in range(2):
                        page(kx[:, n % 2, g * P:(g + 1) * P], I["kidxT"], 2 * n + g, kx_loaded[n % 2])

                def kv_pages(u):
                    if u >= 2:
                        pool.wait_ge(pages_used, u - 1)
                    for g in range(2):
                        page(pg[:, u % 2, g, :], I["kpages"] if u < NS else I["vpages"], 2 * (u % NS) + g,
                             pg_loaded[u % 2])

                pool.wait_ge(pt_loaded, 16)
                low_at(y["c"] + AHEAD)
                kv_pages(0)
                kv_pages(1)
                for c in range(1, 29):
                    if c == 1:
                        index_pages(0)
                        index_pages(1)
                    low_at(y["c"] + c + AHEAD)
                    if c == 6:
                        for n in range(2, NS):
                            index_pages(n)
                    if c >= 16 and c % 2 == 0:
                        kv_pages(c // 2 - 6)
                for u in range(NS + 1, 2 * NS):
                    kv_pages(u)
                split(mixB, 8 * (3 * y["i"] + 1))
                tail = y["c"] + 29
            if y["kind"] == 2:
                pool.wait_ge(x_ready, 16 * y["i"])
                pool.wait_ge(chunk_done, y["c"])
                pool.memset(x4[:], 0.0).then_inc(x4_ready, 1)
                pool.wait_ge(x4_ready, 1)
                for j in range(4):
                    f = slice(32 * j, 32 * j + 32)
                    pool.tensor_copy(x4[f, :, j, :], x[f, :, NP_:N]).then_inc(x4_ready, 1)
                    pool.wait_ge(x4_ready, j + 2)

                def turn_in(t):
                    for a in range(2):
                        pool.wait_ge(turned_ready, t * 4 + (2 * a + 2))
                        pool.wait_ge(g_ready, t * 2)
                        pool.tensor_tensor(uin[:, a, :], turned[:, 2 * a, :], turned[:, 2 * a + 1, :],
                                           (ALU.add, ALU.subtract)[a]).then_inc(u_ready, 1)

                def turn_back(t, s, first=False):
                    pool.wait_ge(g_ready, t * 2 + 2)
                    if not first:
                        pool.wait_ge(y_done, t - 1)
                    pool.tensor_tensor(ph[:, s, 2, :], rot[:, s, 1, :], gst[:, 1, :], ALU.mult).then_inc(ph_pool, 1)
                    pool.tensor_tensor(ph[:, s, 3, :], rot[:, s, 0, :], gst[:, 1, :], ALU.mult).then_inc(ph_pool, 1)
                    pool.wait_ge(ph_pool, t * 2 + 2)
                    pool.wait_ge(ph_dve, t * 2 + 2)
                    for a in range(2):
                        pool.tensor_tensor(s5f[:, a, bass.ds(t, 1)], ph[:, s, a, NP_ - 1:NP_], ph[:, s, 2 + a, NP_ - 1:NP_],
                                           (ALU.subtract, ALU.add)[a]).then_inc(fin_ready, 1)

                turn_in(0)
                for t in range(1, 4):
                    turn_back(t - 1, (t - 1) % 2, t < 3)
                    turn_in(t)
                n0 = 8 * (3 * y["i"] + 1)
                with pool.Fori(1, KT) as i:
                    for j in range(4):
                        turn_back(i * 4 + (j - 1), (j - 1) % 2)
                        turn_in(i * 4 + j)
                    pool.wait_ge(xh_ready, i + n0)
                    low_, src_, high_ = (a[:, bass.ds(i - 1, 1), :].rearrange("p o n -> p (o n)") for a in (xl, mixC, xh))
                    pool.tensor_tensor(low_, src_, high_.bitcast(F32), ALU.subtract).then_inc(xl_ready, 1)
                turn_back(S5T - 1, (S5T - 1) % 2)
                split(mixC, n0, (KT - 1,))
                clear_sums(ln)
                for m in range(KT):
                    low_at(y["c"] + 2 * m + AHEAD)
                    low_at(y["c"] + 2 * m + 1 + AHEAD)
                    square_sum(ln, m)
            else:
                clear_sums(ln)
                for m in range(KT):
                    low_at(tail + m + AHEAD)
                    square_sum(ln, m)
            split(x, 8 * (3 * y["i"] + 2))
            for half in range(2):
                c0 = y["cm"] + 32 * half
                with pool.Fori(0, HHALF // 4) as i:
                    for c in range(4):
                        low(i * 4 + (c0 + c + AHEAD), (c0 + c + AHEAD) % SPL, (c0 + c + AHEAD) % RAW)
                c1 = c0 + HHALF
                if half == 0:
                    with pool.Fori(0, 4) as i:
                        for c in range(4):
                            low(i * 4 + (c1 + c + AHEAD), (c1 + c + AHEAD) % SPL, (c1 + c + AHEAD) % RAW)
                else:
                    clear_sums(ln + 1)
                    for m in range(KT):
                        low_at(c1 + 2 * m + AHEAD)
                        low_at(c1 + 2 * m + 1 + AHEAD)
                        square_sum(ln + 1, m)
            if y["i"] < L - 1:
                split(x, 8 * (3 * y["i"] + 3))

    @block.scalar
    def _(act):
        link = Chain(act, act_link)

        def high(n, s, r_, turn):
            act.wait_ge(raw_loaded[r_], (turn + 1) * 16)
            act.wait_ge(chunk_done, n - SPL + 1)
            act.activation(wh[:, s, :], raw[:, r_, :], ACT.Copy).then_inc(w_high, 1)

        def high_at(n):
            if n >= CHUNKS:
                return
            act.wait_ge(raw_loaded[n % RAW], 16 * (n // RAW + 1))
            if n >= SPL:
                act.wait_ge(chunk_done, n - SPL + 1)
            act.activation(wh[:, n % SPL, :], raw[:, n % RAW, :], ACT.Copy).then_inc(w_high, 1)

        def split(src, n0, ready, r0, ms=range(KT)):
            for m in ms:
                if ready is not None:
                    act.wait_ge(ready, r0 + m + 1)
                act.activation(xh[:, m, :], src[:, m, :], ACT.Copy).then_inc(xh_ready, 1)

        def squares(ln, ready, n, m):
            act.wait_ge(ready, n)
            if m >= 2:
                act.wait_ge(sq_added, 7 * ln + m - 1)
            elif ln:
                act.wait_ge(stats_ready, ln)
            act.activation(lw[:, 2 + m % 2, :], r[:, m, :], ACT.Square).then_inc(sq_ready, 1)

        def finish_norm(ln, y, last):
            act.preload_act_table_set("natural_log_exp_and_others")
            act.wait_ge(var_ready, ln + 1)
            link.step(act.activation(rstd, rstd, ACT.Ln, bias=eps[:, 0:1]))
            act.activation(rstd, rstd, ACT.Exp, scale=-0.5).then_inc(rstd_ready, 1)
            kind = 2 * (ln % 2)
            for m in range(KT):
                act.wait_ge(norm_ready, 8 * ln + m + 1)
                act.activation(x[:, m, :], lw[:, 6 + m % 2, :], ACT.Identity, scale=lnp[:, kind, y["i"], m:m + 1],
                               bias=lnp[:, kind + 1, y["i"], m:m + 1]).then_inc(x_ready, 1)
                if not last:
                    act.wait_ge(x_ready, 8 * ln + m + 1)
                    act.activation(xh[:, m, :], x[:, m, :], ACT.Copy).then_inc(xh_ready, 1)

        for k in range(4):
            act.dma_start(x[:, 2 * k:2 * k + 2, :], I["xT"][:, 2 * k:2 * k + 2, :]).then_inc(x_loaded[k], 16)
        act.dma_start(ident[:], I["ident"]).then_inc(const_loaded, 16)
        act.dma_start(lnp[:], I["lnp"]).then_inc(const_loaded, 16)
        act.dma_start(hgp[:], I["hgp"]).then_inc(const_loaded, 16)
        act.dma_start(lbp[:], I["lbp"]).then_inc(const_loaded, 16)
        act.dma_start(pts[:], I["page_table"]).then_inc(pt_loaded, 16)
        for n in range(AHEAD):
            high_at(n)
        for m in range(KT):
            if m % 2 == 0:
                act.wait_ge(x_loaded[m // 2], 16)
            act.activation(xh[:, m, :], x[:, m, :], ACT.Copy).then_inc(xh_ready, 1)
        act.wait_ge(lb_ready, 1)
        act.activation(lbp[:], lbp[:], ACT.Exp).then_inc(lb_ready, 1)
        act.wait_ge(consts_set, 7)
        act.wait_ge(const_loaded, 64)

        for y in plan:
            ln = 2 * y["i"]
            c0, t0 = y["c"], y["t"]
            if y["kind"] == 0:
                g0 = 8 * y["j"]
                j0 = y["j"]
                if j0:
                    act.wait_ge(chunk_done, c0)
                masks32 = kt[:].bitcast(I32).rearrange("p l t -> p (l t)")[:, 0:LEVELS * NP_ // 2]
                act.dma_start(masks32.rearrange("p (l t) -> p l t", l=LEVELS), I["lmask"]).then_inc(masks_loaded, 16)

                def load_state(h):
                    G = g0 + h
                    if G >= 2:
                        act.wait_ge(s0_stored[G % 2], 16 * (G // 2))
                    act.dma_start(s0b[:, G % 2], I["s_in"][j0, :, h, :, :].rearrange("n k v -> k n v")
                                  ).then_inc(s0_loaded[G % 2], 16)

                def copy_out(h, j):
                    p, T = h % 2, t0 + 4 * h + j
                    act.wait_ge(chunk_done, c0 + 4 * h + j + 1)
                    if j == 0 and h >= 2:
                        act.wait_ge(mix_ready, y["mix"] + h - 1)
                    dst = gt[:, p, :] if j == 3 else fq[:, 4 * p + (0, 2, 3)[j], :]
                    act.activation(halves(dst), lp[:, 2 * (T % 2):2 * (T % 2) + 2, 0:NH2], ACT.Copy).then_inc(tile_out, 1)

                for h in range(HEADS + 1):
                    if h == 0:
                        load_state(0)
                        load_state(1)
                        if t0:
                            act.wait_ge(tile_out, t0)
                        for j in range(4):
                            high_at(c0 + j + AHEAD)
                            copy_out(0, j)
                        continue
                    G, p = g0 + h - 1, (h - 1) % 2
                    f_, k_, q_, v_ = (fq[:, 4 * p + a, :] for a in range(4))
                    act.wait_ge(tile_out, t0 + 4 * h)
                    act.activation(k_, f_, ACT.Sigmoid, scale=-1.0).then_inc(sig_ready, 1)
                    act.wait_ge(sig_ready, 4 * G + 1)
                    act.activation(f_, f_, ACT.Sigmoid).then_inc(sig_ready, 1)
                    if h >= 2:
                        act.wait_ge(mix_ready, y["mix"] + h - 1)
                    act.activation(sgn, q_, ACT.Sigmoid).then_inc(sig_ready, 1)
                    act.wait_ge(gates, G + 1)
                    act.activation(sgn, gt[:, p, :], ACT.Sigmoid).then_inc(sig_ready, 1)
                    def between(j):
                        if h < HEADS:
                            copy_out(h, j)
                            high_at(c0 + 4 * h + j + AHEAD)
                        else:
                            split(mixA, 8 * (3 * y["i"] + 1), mix_ready, y["mix"], (range(3), range(3, 7), ())[j - 1])

                    if h < HEADS:
                        copy_out(h, 0)
                    act.preload_act_table_set("natural_log_exp_and_others")
                    act.wait_ge(f_ready, 2 * G + 2)
                    act.activation(lf[:, 0:NP_], f_[:, 0:NP_], ACT.Ln).then_inc(lf_ready, 1)
                    act.wait_ge(b_ready, G + 1)
                    act.activation(lf[:, 0:NP_], bb[:, 0:NP_], ACT.Exp).then_inc(eb_ready, 1)
                    if h < HEADS:
                        high_at(c0 + 4 * h + AHEAD)
                    for l in range(LEVELS + 1):
                        act.wait_ge(d_ready, 8 * G + l + 1)
                        if l == 2:
                            act.wait_ge(kp_ready, G + 1)
                        elif 7 * G + l - 2 > 0:
                            act.wait_ge(kt_ready, 7 * G + l - 2 if l > 2 else 7 * G - 1 + l)
                        if 8 * G + l >= 2:
                            act.wait_ge(qt_ready, 8 * G + l - 1)
                        act.activation(ee[:, l % 2, :], dd[:, l % 2, :], ACT.Exp).then_inc(e_ready, 1)
                        if l == 1:
                            between(1)
                        if l == 6 and 2 <= h < HEADS:
                            load_state(h)
                        if l == 4:
                            act.wait_ge(tok_ready, G + 1)
                            act.activation(ktok[:], mb[:, 0, :], ACT.Copy).then_inc(tok_copied, 1)
                            act.activation(vtok[:], mb[:, 1, :], ACT.Copy).then_inc(tok_copied, 1)
                            if G:
                                act.wait_ge(su_ready, G)
                            act.activation(tok8[:].rearrange("n a d -> n (a d)"), mb[0:NS, 2, 0:2 * P], ACT.Copy).then_inc(tok_copied, 1)
                    between(2)
                    act.wait_ge(o_ready, G + 1)
                    act.activation(ot[:, 0:NP_], mb[:, 0, :], ACT.Copy).then_inc(act_link, 1)
                    act.wait_ge(so_ready, G + 1)
                    act.activation(ot[:, NP_:N], mb[:, 1, 0:NS], ACT.Copy).then_inc(act_link, 1)
                    link.n += 2
                    link.wait()
                    act.activation(osq, ot, ACT.Square).then_inc(osq_ready, 1)
                    act.wait_ge(ms_ready, G + 1)
                    link.step(act.activation(halves(orstd), mb[:, 2:4, 0:NH2], ACT.Ln, bias=eps[:, 1:2]))
                    act.activation(orstd, orstd, ACT.Exp, scale=-0.5).then_inc(orstd_ready, 1)
                    between(3)
                    act.wait_ge(states_ready, G + 1)
                    act.dma_start(O["hg_p"][j0, h - 1, :, :], st[:, 3 + p, :]).then_inc(st_stored, 16)
                    act.wait_ge(so_ready, G + 1)
                    act.dma_start(O["hg_s"][j0, :, h - 1, :, :].rearrange("n k v -> k n v"), s0b[:, G % 2]
                                  ).then_inc(s0_stored[G % 2], 16)
                split(mixA, 8 * (3 * y["i"] + 1), mix_ready, y["mix"], (KT - 1,))
                tail, ttail = c0 + 32, t0 + 32
            if y["kind"] == 1:
                for dst, src in ((kiln[:], "kiln"), (ones_idx[:], "ones_idx"), (cmask[:], "cmask"), (wwi, "wwi"),
                                 (relb[:], "relb"), (oh_p[:], "oh_p"), (rep8, "rep8"), (oh4, "oh4")):
                    act.dma_start(dst, I[src]).then_inc(b_loaded, 16)

                def copy_tile(c, dst, **kw):
                    act.wait_ge(chunk_done, c0 + c + 1)
                    T = t0 + c
                    act.activation(halves(dst), lp[:, 2 * (T % 2):2 * (T % 2) + 2, 0:NH2], ACT.Copy, **kw
                                   ).then_inc(tile_out, 1)

                def scores(u):
                    qb, h = IUNITS[u]
                    w = (qb + 1) * P
                    act.wait_ge(dot_ready, u + 1)
                    if u >= 2:
                        act.wait_ge(score_added, u - 1)
                    act.activation(rl[:, u % 2, 0:w], mb[:, u % 4, 0:w], ACT.Relu, scale=IDX_DIM ** -0.5
                                   ).then_inc(relu_done, 1)

                act.preload_act_table_set("natural_log_exp_and_others")
                act.wait_ge(tile_out, t0)
                high_at(c0 + AHEAD)
                copy_tile(0, kiT)
                act.wait_ge(tile_out, t0 + 1)
                act.activation(rl[:, 0, :], kiT, ACT.Square).then_inc(ki_raw, 1)
                for c in range(1, 5):
                    high_at(c0 + c + AHEAD)
                    copy_tile(c, qi[:, c - 1, :])
                    if c == 1:
                        act.wait_ge(ki_var, 1)
                        link.step(act.activation(pt_[:, 0, :], pt_[:, 0, :], ACT.Ln, bias=eps[:, 0:1]))
                        act.activation(pt_[:, 0, :], pt_[:, 0, :], ACT.Exp, scale=-0.5).then_inc(ki_rstd, 1)
                        act.wait_ge(ki_norm, 1)
                        act.wait_ge(b_loaded, 16 * 8)
                        act.activation(kiT, kiT, ACT.Identity, scale=kiln[:, 0:1], bias=kiln[:, 1:2]).then_inc(ki_ready, 1)
                        act.wait_ge(ki_ready, 1)
                        act.dma_start(O["kidxT"], kiT[0:IDX_DIM, :]).then_inc(kv_stored, 16)
                act.wait_ge(wi_psum, 1)
                act.activation(wtk[:, 1:TB, :], mb[:, 0, 0:3 * IH].rearrange("p (b h) -> p b h", h=IH), ACT.Copy,
                               scale=IH ** -0.5).then_inc(wi_ready, 1)
                act.activation(wi8, mb[0:4, 1, 0:2 * NS], ACT.Copy, scale=IH ** -0.5).then_inc(wi_ready, 1)
                act.wait_ge(rows_ready, 1)
                act.activation(rowb[:, 0:512], mb[0:HEADS, 2, :], ACT.Copy).then_inc(rows_out, 1)
                act.activation(rowb[:, 512:ROW], mb[0:HEADS, 3, 0:ROW - 512], ACT.Copy).then_inc(rows_out, 1)
                act.wait_ge(rows_out, 2)
                act.dma_start(bias_rows, rowb.unsqueeze(1).to_broadcast([HEADS, P, ROW])).then_inc(rows_stored, 16)

                def load_bias(h):
                    if h >= 2:
                        act.wait_ge(l_ready, TB * (h - 1))
                    elif h == 0:
                        act.wait_ge(rows_stored, 16)
                        for s in v_stored:
                            act.wait_ge(s, 16 * HEADS // 2)
                    flat = bias_rows[h, :, :].rearrange("p i -> (p i)")
                    act.dma_start(tb[:, h % 2, :], flat[P - 1:P - 1 + P * (ROW - 1)].rearrange("(p i) -> p i", i=ROW - 1)[:, 0:NP_]
                                  ).then_inc(tb_loaded[h % 2], 16)

                order = list(range(5, 29))
                for c in order[:2]:
                    high_at(c0 + c + AHEAD)
                    copy_tile(c, mixB[:, c - 5, :])
                for u in range(len(IUNITS)):
                    scores(u)
                for n in range(NS):
                    act.wait_ge(sdot_ready, n + 1)
                    if n:
                        act.wait_ge(s8_ready, n)
                    act.activation(srl, mb[0:4, 0:2, 0:SK], ACT.Relu, scale=IDX_DIM ** -0.5).then_inc(srelu_done, 1)
                act.wait_ge(s8_ready, NS)
                act.activation(s8, mb[0:NS, 2, 0:SK], ACT.Copy).then_inc(s8_out, 1)
                for c in order[2:]:
                    high_at(c0 + c + AHEAD)
                    if c < 13:
                        copy_tile(c, mixB[:, c - 5, :])
                    elif c < 21:
                        copy_tile(c, kT[:, c - 13, :])
                        if c == 20:
                            act.wait_ge(tile_out, t0 + 21)
                            act.dma_start(O["kT"], kT[:]).then_inc(kv_stored, 16)
                    else:
                        h = c - 21
                        if h >= 2:
                            act.wait_ge(vtr_ready, h - 1)
                            act.wait_ge(v_stored[h % 2], 16 * (h // 2))
                        copy_tile(c, vT[:, h % 2, :])
                        act.wait_ge(tile_out, t0 + c + 1)
                        act.dma_start(O["vT"][:, h, :], vT[:, h % 2, :]).then_inc(v_stored[h % 2], 16)
                        link.mark(act.activation(vs8[:, h, :], vT[:, h % 2, NP_:N], ACT.Copy))
                        act.wait_ge(vtr_ready, h + 1)
                        act.activation(vtk[:, :, h, :], mb[:, h % 2, :].rearrange("p (b d) -> p b d", d=P), ACT.Copy
                                       ).then_inc(vtr_out, 1)
                load_bias(0)
                load_bias(1)
                act.wait_ge(spsum, 1)
                act.activation(ltok, mb[:, 3, 0:P], ACT.Copy).then_inc(slog, 1)
                act.wait_ge(sz_ready, 1)
                act.activation(zb, mb[0:HN, 2, 0:SK], ACT.Copy).then_inc(sz_out, 1)
                act.wait_ge(sl_ready, 1)
                act.activation(sl, sl, ACT.Exp, bias=a_small[0:HN, 1:2], accum_out=a_small[0:HN, 2:3]).then_inc(sexp, 1)
                act.wait_ge(spt_ready, 1)
                act.activation(sptt, mb[:, 3, 0:P], ACT.Copy).then_inc(spt_out, 1)
                act.activation(sbc, mb[:, 1, 0:HN], ACT.Copy).then_inc(sbc_out, 1)
                for u in range(len(UNITS) + 1):
                    if u < len(UNITS):
                        h, qb = UNITS[u]
                        w = (qb + 1) * P
                        act.wait_ge(l_ready, u + 1)
                        act.activation(pb_[:, u % 2, 0:w], pb_[:, u % 2, 0:w], ACT.Exp, bias=nmx(u), accum_out=sme(u)
                                       ).then_inc(exp_done, 1)
                    if u:
                        h, qb = UNITS[u - 1]
                        w = (qb + 1) * P
                        act.wait_ge(ptr_ready, u)
                        if u >= 3:
                            act.wait_ge(pv_ready, u - 2)
                        act.activation(pt_[:, (u - 1) % 2, 0:w], mb[:, 2 + (u - 1) % 2, 0:w], ACT.Copy).then_inc(ptr_out, 1)
                        if qb == TB - 1:
                            act.wait_ge(pv_ready, u)
                            act.activation(mixB[:, h, 0:NP_], lp[:, h % 2, :], ACT.Copy).then_inc(pv_out, 1)
                            if h + 2 < HEADS:
                                load_bias(h + 2)
                act.wait_ge(pv_out, HEADS)
                act.wait_ge(mix_ready, y["mix"] + 1)
                split(mixB, 8 * (3 * y["i"] + 1), None, 0)
                tail, ttail = c0 + 29, t0 + 29
            if y["kind"] == 2:
                act.wait_ge(x_ready, 16 * y["i"])
                act.wait_ge(chunk_done, c0)
                for dst, src in ((s5v[:, 0:3, :], "s5_ab"), (braw, "s5_b"), (cmat[:, 0:2], "s5_c"), (s5s[:], "s5_s"),
                                 (s5d[:], "s5_d"), (s5g[:], "s5_g")):
                    act.dma_start(dst, I[src]).then_inc(s5_loaded, 16)
                act.wait_ge(s5_loaded, 16 * 6)
                act.activation(s5v[:, 2, :], s5v[:, 2, :], ACT.Exp).then_inc(s5_dt, 1)
                act.wait_ge(s5_arg, 1)
                act.activation(s5v[:, 3, :], s5v[:, 3, :], ACT.Exp).then_inc(s5_mag, 1)
                act.wait_ge(s5_red, 1)
                act.activation(ang[:, 2], ang[:, 2], ACT.Sin).then_inc(s5_sin, 1)
                act.activation(ang[:, 3], ang[:, 3], ACT.Sin).then_inc(s5_sin, 1)

                def spin(t, s):
                    for q, (a, b) in enumerate(((0, 0), (1, 1), (1, 0), (0, 1))):
                        if q == 0:
                            act.wait_ge(first_ready, t * 2 + 2)
                        if t:
                            act.wait_ge(rot_ready, t * 2 - 1 + q // 2)
                        for n in range(3):
                            ins = act.activation(spun[:, q, n, :], rot[:, s, a, 0:P], ACT.Copy,
                                                 scale=top[:, b, bass.ds(t, 1), n + 1])
                        ins.then_inc(spun_ready, 1)

                def gelu(m):
                    mk, hk = (a[:, bass.ds(m, 1), :].rearrange("p o n -> p (o n)") for a in (mixC, xh))
                    act.wait_ge(gin_ready, m * 2 + 2)
                    act.activation(mk, mk, ACT.Gelu_apprx_tanh).then_inc(mix_ready, 1)
                    act.wait_ge(mix_ready, m + (y["mix"] + 1))
                    act.activation(hk, mk, ACT.Copy).then_inc(xh_ready, 1)

                for t in range(4):
                    spin(t, t % 2)
                act.wait_ge(s5h_ready, 2)
                act.dma_start(O["s5_s"], s5h[:]).then_inc(s5_stored, 16)
                for k in range(1, KT):
                    for j in range(4):
                        spin(k * 4 + j, j % 2)
                    gelu(k - 1)
                gelu(KT - 1)
                act.wait_ge(fin_ready, 2 * S5T)
                act.dma_start(O["s5_p"], s5f[:]).then_inc(s5_stored, 16)
                act.wait_ge(tile_out, t0)

                for m in range(KT):
                    for a in range(2):
                        T = t0 + 2 * m + a
                        high_at(c0 + 2 * m + a + AHEAD)
                        act.wait_ge(chunk_done, c0 + 2 * m + a + 1)
                        if m >= 2:
                            act.wait_ge(glu_done, m - 1)
                        act.activation(halves(lw[:, 4 + 2 * a + m % 2, :]), lp[:, 2 * (T % 2):2 * (T % 2) + 2, 0:NH2],
                                       (ACT.Identity, ACT.Sigmoid)[a], bias=s5g[:, KT * a + m:KT * a + m + 1]
                                       ).then_inc(tile_out, 1)
                    if m:
                        squares(ln, glu_done, m, m - 1)
                squares(ln, glu_done, KT, KT - 1)
                act.wait_ge(s5_stored, 32)
            else:
                for m in range(KT):
                    high_at(tail + m + AHEAD)
                    squares(ln, tile_out, ttail + m + 1, m)
            if y["kind"] == 1:
                act.wait_ge(kv_stored, 32)
            if y["kind"] == 0:
                for stored_ in s0_stored:
                    act.wait_ge(stored_, 16 * (g0 + HEADS) // 2)
                act.wait_ge(st_stored, 16 * (g0 + HEADS))
            finish_norm(ln, y, False)
            for half in range(2):
                c1, t1 = y["cm"] + 32 * half, y["tm"] + 24 * half
                g1 = HHALF * (2 * y["i"] + half)
                act.wait_ge(tile_out, t1)

                def hidden(i):
                    for c in range(4):
                        n = c1 + c + AHEAD
                        high(i * 4 + n, n % SPL, n % RAW, i * (4 // RAW) + n // RAW)
                        T = t1 + c
                        act.wait_ge(chunk_done, i * 4 + (c1 + c + 1))
                        if g1 or not isinstance(i, int) or c >= 2:
                            act.wait_ge(h_ready, i * 4 + (g1 + c - 1))
                        act.activation(halves(lw[:, 6 + c % 2, :]), lp[:, 2 * (T % 2):2 * (T % 2) + 2, 0:NH2], ACT.Relu
                                       ).then_inc(tile_out, 1)

                hidden(0)
                with act.Fori(1, HHALF // 4) as i:
                    hidden(i)
                c1, t1 = c1 + HHALF, t1 + HHALF
                if half == 0:
                    with act.Fori(0, 4) as i:
                        for c in range(4):
                            n = c1 + c + AHEAD
                            high(i * 4 + n, n % SPL, n % RAW, i * (4 // RAW) + n // RAW)
                else:
                    for m in range(KT):
                        high_at(c1 + 2 * m + AHEAD)
                        high_at(c1 + 2 * m + 1 + AHEAD)
                        squares(ln + 1, tile_out, t1 + m + 1, m)
            finish_norm(ln + 1, y, y["i"] == L - 1)
        act.wait_ge(pt_loaded, 16)
        if 1 in kinds:
            act.wait_ge(kv_stored, 32)
        if 0 in kinds:
            act.wait_ge(st_stored, 16 * 8 * kinds.count(0))
            for stored_ in s0_stored:
                act.wait_ge(stored_, 16 * 4 * kinds.count(0))

    @block.vector
    def _(dve):
        link = Chain(dve, dve_link)

        def add_sum(m):
            if m == 0:
                link.step(dve.tensor_copy(rsum, r[:, 0, :]))
            elif m < KT - 2:
                link.step(dve.tensor_tensor(rsum, rsum, r[:, m, :], ALU.add))
            elif m == KT - 2:
                dve.tensor_tensor(rsum, rsum, r[:, m, :], ALU.add).then_inc(sum_ready, 1)

        def residual(n, T, m, mh):
            dve.wait_ge(chunk_done, n + 1)
            src = lp[:, 2 * (T % 2):2 * (T % 2) + 2, 0:NH2]
            if mh == "second":
                dve.tensor_tensor(halves(r[:, m, :]), halves(r[:, m, :]), src, ALU.add).then_inc(tile_out, 1)
            else:
                dve.scalar_tensor_tensor(halves(r[:, m, :]), halves(x[:, m, :]), ALPHA, src, ALU.mult, ALU.add
                                         ).then_inc(tile_out, 1)
            if mh != "first":
                dve.wait_ge(tile_out, T + 1)
                add_sum(m)

        def level(G, l, k_, q_):
            m = 1 << (l - 1)
            dve.wait_ge(e_ready, 8 * G + l + 1)
            if G:
                dve.wait_ge(att_ready, 8 * (G - 1) + l + 1)
            dve.tensor_tensor(kt[:, l - 1, :], k_[:, 0:NP_], ee[:, l % 2, :], ALU.mult).then_inc(kt_ready, 1)
            dve.tensor_tensor(qt[:, l - 1, :].rearrange("p (c t) -> p c t", t=m),
                              q_[:, 0:NP_].rearrange("p (c a t) -> p c a t", a=2, t=m)[:, :, 1, :],
                              ee[:, l % 2, :].rearrange("p (c a t) -> p c a t", a=2, t=m)[:, :, 1, :], ALU.mult
                              ).then_inc(qt_ready, 1)

        def merge(G, l):
            m = 1 << (l - 1) if l else 0
            dve.wait_ge(att_ready, 8 * G + l + 1)
            if l == 0:
                dve.tensor_tensor(att[:].rearrange("p (c t) -> p c t", t=P),
                                  mb[:, 3, :].rearrange("p (c t) -> p c t", t=P),
                                  ident[:].unsqueeze(1).to_broadcast([P, TB, P]), ALU.mult).then_inc(att_merged, 1)
                return
            if l == 1:
                dve.wait_ge(tok_copied, 3 * (G + 1))
            dve.wait_ge(att_merged, 8 * G + l)
            right = att[:].rearrange("p (c a t) -> p c a t", a=2, t=m)[:, :, 1, :]
            bank = mb[:, 2 if l % 2 else 3, 0:NP_ // 2]
            dve.copy_predicated(right, lmask[:, l - 1, :].rearrange("p (c t) -> p c t", t=m),
                                bank.rearrange("p (c t) -> p c t", t=m)).then_inc(att_merged, 1)

        def norm(ln, y):
            dve.wait_ge(stats_ready, ln + 1)
            link.step(dve.tensor_copy(halves(mean), mb[:, 0:2, 0:NH2]))
            link.step(dve.tensor_tensor(lw[:, 6, :], mean, mean, ALU.mult))
            dve.tensor_tensor(halves(rstd), mb[:, 2:4, 0:NH2], halves(lw[:, 6, :]), ALU.subtract).then_inc(var_ready, 1)
            for m in range(KT):
                if m == 0:
                    dve.wait_ge(var_ready, ln + 1)
                else:
                    dve.wait_ge(x_ready, 8 * ln + m - 1)
                link.step(dve.tensor_tensor(lw[:, 6 + m % 2, :], r[:, m, :], mean, ALU.subtract))
                if m == 0:
                    dve.wait_ge(rstd_ready, ln + 1)
                dve.tensor_tensor(lw[:, 6 + m % 2, :], lw[:, 6 + m % 2, :], rstd, ALU.mult).then_inc(norm_ready, 1)

        dve.wait_ge(consts_set, 7)
        dve.wait_ge(const_loaded, 64)
        link.step(dve.tensor_tensor(lbt[:, 0, :], lbp[:, 0, :], lbp[:, 1, :], ALU.max))
        link.step(dve.tensor_tensor(lbt[:, 1, :], lbp[:, 2, :], lbp[:, 3, :], ALU.max))
        link.step(dve.tensor_tensor(lbt[:, 0, :], lbt[:, 0, :], lbt[:, 1, :], ALU.max))
        dve.tensor_tensor(lbp[:], lbp[:], lbt[:, 0:1, :].to_broadcast([P, DEPTH, KT]), ALU.subtract).then_inc(lb_ready, 1)
        dve.wait_ge(lb_ready, 2)
        link.step(dve.tensor_tensor(lbt[:, 0, :], lbp[:, 0, :], lbp[:, 1, :], ALU.add))
        link.step(dve.tensor_tensor(lbt[:, 0, :], lbt[:, 0, :], lbp[:, 2, :], ALU.add))
        link.step(dve.tensor_tensor(lbt[:, 0, :], lbt[:, 0, :], lbp[:, 3, :], ALU.add))
        link.step(dve.reciprocal(lbt[:, 1, :], lbt[:, 0, :]))
        link.step(dve.tensor_tensor(lbp[:], lbp[:], lbt[:, 1:2, :].to_broadcast([P, DEPTH, KT]), ALU.mult))
        for j in range(2):
            i = 3 * j
            link.step(dve.tensor_copy(lb[:, j, 0, :], lbp[:, 0, :]))
            for a in range(1, i + 1):
                link.step(dve.tensor_tensor(lb[:, j, 0, :], lb[:, j, 0, :], lbp[:, a, :], ALU.add))
            link.step(dve.tensor_tensor(lb[:, j, 0, :], lb[:, j, 0, :], lbp[:, 0, :], ALU.subtract))
            link.step(dve.tensor_scalar(lb[:, j, 1, :], lb[:, j, 0, :], -1.0, 1.0, ALU.mult, ALU.add))

        for y in plan:
            ln = 2 * y["i"]
            c0, t0 = y["c"], y["t"]
            if y["kind"] == 0:
                g0, jj = 8 * y["j"], y["j"]
                dve.wait_ge(masks_loaded, 16 * (y["j"] + 1))
                masks32 = kt[:].bitcast(I32).rearrange("p l t -> p (l t)")[:, 0:LEVELS * NP_ // 2]
                link.step(dve.tensor_copy(lmask[:].rearrange("p l t -> p (l t)"), masks32))
                for h in range(HEADS):
                    G, p = g0 + h, h % 2
                    f_, k_, q_, v_ = (fq[:, 4 * p + a, :] for a in range(4))
                    g_ = gt[:, p, :]
                    dve.wait_ge(sig_ready, 4 * G + 2)
                    dve.tensor_scalar(k_, k_, lb[:, jj, 1, h:h + 1], None, ALU.mult).then_inc(f_ready, 1)
                    dve.wait_ge(f_ready, 2 * G + 1)
                    dve.tensor_scalar(f_, f_, lb[:, jj, 1, h:h + 1], lb[:, jj, 0, h:h + 1], ALU.mult, ALU.add
                                      ).then_inc(f_ready, 1)
                    dve.wait_ge(sig_ready, 4 * G + 3)
                    dve.tensor_tensor(q_, q_, sgn, ALU.mult).then_inc(gates, 1)
                    dve.wait_ge(lf_ready, G + 1)
                    dve.tensor_tensor_scan(bb[:, 0:NP_], keep[:], lf[:, 0:NP_], 0.0, ALU.mult, ALU.add).then_inc(b_ready, 1)
                    dve.wait_ge(sig_ready, 4 * G + 4)
                    link.step(dve.scalar_tensor_tensor(g_, g_, hgp[:, jj, h:h + 1], sgn, ALU.mult, ALU.mult))
                    dve.wait_ge(b_ready, G + 1)
                    for l in range(LEVELS + 1):
                        n = 8 * G + l
                        if n >= 2:
                            dve.wait_ge(e_ready, n - 1)
                        s = dd[:, l % 2, :]
                        if l == 0:
                            end = bb[:, P - 1:NP_:P].unsqueeze(2).to_broadcast([P, TB, P])
                            dve.tensor_tensor(s.rearrange("p (c t) -> p c t", t=P), end,
                                              bb[:, 0:NP_].rearrange("p (c t) -> p c t", t=P), ALU.subtract
                                              ).then_inc(d_ready, 1)
                        else:
                            m = 1 << (l - 1)
                            b4 = bb[:, 0:NP_].rearrange("p (c a t) -> p c a t", a=2, t=m)
                            s4 = s.rearrange("p (c a t) -> p c a t", a=2, t=m)
                            mid = b4[:, :, 0, m - 1:m].to_broadcast([P, NP_ // (2 * m), m])
                            link.mark(dve.tensor_tensor(s4[:, :, 0, :], mid, b4[:, :, 0, :], ALU.subtract))
                            dve.tensor_tensor(s4[:, :, 1, :], b4[:, :, 1, :], mid, ALU.subtract).then_inc(d_ready, 1)
                            link.wait()
                        if l == 0:
                            dve.wait_ge(eb_ready, G + 1)
                            dve.wait_ge(gates, G + 1)
                            if G:
                                dve.wait_ge(o_ready, G)
                            dve.tensor_tensor(qe[:], q_[:, 0:NP_], lf[:, 0:NP_], ALU.mult).then_inc(qt_ready, 1)
                        if l >= 2:
                            level(G, l - 1, k_, q_)
                        if l >= 5:
                            merge(G, l - 5)
                    level(G, LEVELS, k_, q_)
                    for l in range(3, LEVELS + 1):
                        merge(G, l)
                        if l == 5:
                            if G:
                                dve.wait_ge(su_ready, G)
                            dve.tensor_tensor(vz[:], tok8[:, 1:2, :].to_broadcast([NS, NS, P]),
                                              ident[0:NS, 0:NS].unsqueeze(2).to_broadcast([NS, NS, P]), ALU.mult
                                              ).then_inc(vz_ready, 1)
                    dve.wait_ge(upd_ready, G + 1)
                    if G >= 2:
                        dve.wait_ge(st_stored, 16 * (G - 1))
                    link.step(dve.tensor_copy(st[:, 0, :], mb[:, 1, 0:P]))
                    for c in range(1, TB):
                        ins = dve.scalar_tensor_tensor(st[:, c if c < TB - 1 else 3 + p, :], st[:, c - 1, :],
                                                       lf[:, (c + 1) * P - 1:(c + 1) * P], mb[:, 1, c * P:(c + 1) * P], ALU.mult, ALU.add)
                        if c < TB - 1:
                            link.step(ins)
                    ins.then_inc(states_ready, 1)
                    dve.wait_ge(su_ready, G + 1)
                    dve.wait_ge(sf_ready, G + 1)
                    dve.tensor_tensor(s0b[:, G % 2], s0b[:, G % 2], mb[:, 2:4, :].rearrange("p b (n d) -> p (b n) d", d=P), ALU.add
                                      ).then_inc(snew_ready, 1)
                    dve.wait_ge(orstd_ready, G + 1)
                    link.step(dve.tensor_tensor(ot, ot, orstd, ALU.mult))
                    dve.tensor_tensor(mixA[:, h, :], ot, g_, ALU.mult).then_inc(mix_ready, 1)
                tail, ttail = c0 + 32, t0 + 32
            if y["kind"] == 1:
                dve.wait_ge(ki_stats, 1)
                km, kv_, t_ = pt_[:, 1, :], pt_[:, 0, :], rl[:, 1, :]
                link.step(dve.tensor_copy(halves(km), mb[:, 0:2, 0:NH2]))
                link.step(dve.tensor_tensor(t_, km, km, ALU.mult))
                dve.tensor_tensor(halves(kv_), mb[:, 2:4, 0:NH2], halves(t_), ALU.subtract).then_inc(ki_var, 1)
                link.step(dve.tensor_tensor(kiT, kiT, km, ALU.subtract))
                dve.wait_ge(ki_rstd, 1)
                dve.tensor_tensor(kiT, kiT, kv_, ALU.mult).then_inc(ki_norm, 1)
                dve.wait_ge(wi_ready, 2)
                for a in range(2):
                    dve.tensor_tensor(w3[:, a, :, :], oh4.rearrange("k (n m) -> k n m", n=NS),
                                      wi8[:, a * NS:(a + 1) * NS].unsqueeze(2).to_broadcast([4, NS, NS]), ALU.mult
                                      ).then_inc(w3_ready, 1)
                for u, (qb, h) in enumerate(IUNITS):
                    w = (qb + 1) * P
                    wcol = wtk[:, qb, (h % 2) * 4 + h // 2:(h % 2) * 4 + h // 2 + 1]
                    dve.wait_ge(relu_done, u + 1)
                    if h:
                        dve.wait_ge(score_added, u)
                        ins = dve.scalar_tensor_tensor(sc[:, qb, 0:w], rl[:, u % 2, 0:w], wcol, sc[:, qb, 0:w],
                                                       ALU.mult, ALU.add)
                    else:
                        ins = dve.tensor_scalar(sc[:, qb, 0:w], rl[:, u % 2, 0:w], wcol, None, ALU.mult)
                    ins.then_inc(score_added, 1)
                for n in range(NS):
                    if n >= 2:
                        dve.wait_ge(sdot_ready, n - 1)
                    dve.wait_ge(ki_ready, 1)
                    dve.tensor_copy(kx[:, n % 2, PAST:SK], kiT[:, NP_ + n:NP_ + n + 1]).then_inc(kx_own, 1)
                dve.wait_ge(score_added, len(IUNITS))
                dve.wait_ge(b_loaded, 16 * 8)

                def select(a, k):
                    rows = a.shape[0]
                    for _ in range(k // 8):
                        link.step(dve.max(top8[0:rows, :], a))
                        link.step(dve.match_replace(a, top8[0:rows, :], a, TAKEN))
                    return dve.tensor_scalar(a, a, TAKEN / 2, NEG, ALU.is_gt, ALU.mult)

                dve.wait_ge(s8_out, 1)
                select(s8, SSEL).then_inc(sneg_ready, 1)
                dve.tensor_copy(sc[:, 0, 0:P], cmask[:]).then_inc(top_done, 1)
                for qb in range(1, TB):
                    link.step(dve.tensor_tensor(sc[:, qb, qb * P:(qb + 1) * P], sc[:, qb, qb * P:(qb + 1) * P], cmask[:], ALU.add))
                    select(sc[:, qb, 0:(qb + 1) * P], PSEL).then_inc(top_done, 1)
                dve.wait_ge(rows_stored, 16)
                dve.wait_ge(tile_out, t0 + 21)
                dve.tensor_tensor(sprodt.rearrange("p (h n) -> p h n", h=HEADS), mixB[:, :, NP_:N], kT[:, :, NP_:N], ALU.mult
                                  ).then_inc(sprod, 1)
                dve.wait_ge(sy_ready, 1)
                dve.wait_ge(sz_out, 1)
                link.step(dve.scalar_tensor_tensor(sl, mb[0:HN, 1, 0:SK], DH ** -0.5, zb, ALU.mult, ALU.add))
                link.step(dve.reduce_max(s_small[0:HN, 0:1], sl, AX.X))
                dve.tensor_scalar(a_small[0:HN, 1:2], s_small[0:HN, 0:1], -1.0, None, ALU.mult).then_inc(sl_ready, 1)
                dve.wait_ge(sexp, 1)
                link.step(dve.reciprocal(s_small[0:HN, 1:2], a_small[0:HN, 2:3]))
                link.step(dve.tensor_scalar(sl, sl, s_small[0:HN, 1:2], None, ALU.mult))
                dve.tensor_scalar(sdiag, ident[0:HN, 0:HN], sl[:, PAST:SK], None, ALU.mult).then_inc(sp_ready, 1)
                dve.wait_ge(top_done, TB)
                for u in range(len(UNITS) + 1):
                    if u < len(UNITS):
                        h, qb = UNITS[u]
                        w = (qb + 1) * P
                        pw = pb_[:, u % 2, 0:w]
                        dve.wait_ge(log_ready, u + 1)
                        if u >= 2:
                            dve.wait_ge(ptr_ready, u - 1)
                        if qb == 0:
                            dve.wait_ge(tb_loaded[h % 2], 16 * (h // 2 + 1))
                        off = P * (TB - 1 - qb)
                        link.step(dve.scalar_tensor_tensor(pw, mb[:, u % 2, 0:w], DH ** -0.5, tb[:, h % 2, off:off + w],
                                                           ALU.mult, ALU.add))
                        link.step(dve.tensor_tensor_reduce(out=pw, in0=pw, in1=sc[:, qb, 0:w], scale=1.0, scalar=3 * NEG,
                                                           op0=ALU.add, op1=ALU.max, accum_out=s_small[:, 2:3]))
                        dve.tensor_scalar(nmx(u), s_small[:, 2:3], -1.0, None, ALU.mult).then_inc(l_ready, 1)
                    if u:
                        h, qb = UNITS[u - 1]
                        w = (qb + 1) * P
                        pw = pb_[:, (u - 1) % 2, 0:w]
                        dve.wait_ge(exp_done, u)
                        dve.wait_ge(p_ready, u - 1)
                        link.step(dve.reciprocal(s_small[:, 3:4], sme(u - 1)))
                        dve.tensor_scalar(pw, pw, s_small[:, 3:4], None, ALU.mult).then_inc(p_ready, 1)
                dve.wait_ge(pages_used, 2 * NS)
                dve.wait_ge(sbc_out, 1)
                link.step(dve.tensor_tensor(vs8, vs8, sbc.rearrange("p (h n) -> p h n", h=HEADS), ALU.mult))
                dve.tensor_tensor(mixB[:, :, NP_:N], lp[:, 2, 0:HN].rearrange("p (h n) -> p h n", h=HEADS),
                                  vs8, ALU.add).then_inc(mix_ready, 1)
                tail, ttail = c0 + 29, t0 + 29
            if y["kind"] == 2:
                ar, ai, dt, mag, abr, abi, nr, den, ta, tb_, zr, zi = (s5v[:, a, :] for a in range(12))

                def mul(out, a, b):
                    link.mark(dve.tensor_tensor(out, a, b, ALU.mult))

                def cmul(out, a, b, tmp, conj=False):
                    mul(tmp[0], a[0], b[0])
                    mul(tmp[1], a[1], b[1])
                    mul(tmp[2], a[1], b[0])
                    mul(tmp[3], a[0], b[1])
                    link.wait()
                    link.mark(dve.tensor_tensor(out[0], tmp[0], tmp[1], ALU.subtract))
                    link.step(dve.tensor_tensor(out[1], tmp[2], tmp[3], ALU.add))

                dve.wait_ge(s5_loaded, 16 * 6)
                dve.wait_ge(s5_dt, 1)
                mul(ang[:, 0, 0, :], dt, ai)
                dve.tensor_tensor(mag, dt, ar, ALU.mult).then_inc(s5_arg, 1)
                link.wait()
                for m in range(1, ANG):
                    link.mark(dve.tensor_scalar(ang[:, 0, m, :], ang[:, 0, 0, :], float(1 << m), None, ALU.mult))
                link.wait()
                th, turns, si, co = (ang[:, a] for a in range(4))
                link.step(dve.tensor_scalar(turns, th, 1 / (2 * math.pi), ROUND, ALU.mult, ALU.add))
                link.step(dve.tensor_scalar(turns, turns, ROUND, None, ALU.subtract))
                link.step(dve.scalar_tensor_tensor(si, turns, -TURN_HI, th, ALU.mult, ALU.add))
                link.step(dve.scalar_tensor_tensor(si, turns, -TURN_LO, si, ALU.mult, ALU.add))
                link.step(dve.tensor_scalar(si, si, PI32, -PI32, ALU.min, ALU.max))
                link.step(dve.scalar_tensor_tensor(co, si, -1.0, si, ALU.mult, ALU.max))
                dve.tensor_scalar(co, co, -1.0, math.pi / 2, ALU.mult, ALU.add).then_inc(s5_red, 1)
                mul(ta, ar, ar)
                mul(tb_, ai, ai)
                link.wait()
                link.step(dve.tensor_tensor(den, ta, tb_, ALU.add))
                link.step(dve.reciprocal(den, den))
                dve.wait_ge(s5_sin, 2)
                dve.wait_ge(s5_mag, 1)
                mul(abr, mag, co[:, 0, :])
                mul(abi, mag, si[:, 0, :])
                link.wait()
                link.step(dve.tensor_scalar(nr, abr, 1.0, None, ALU.subtract))
                mul(ta, nr, ar)
                mul(tb_, abi, ai)
                link.wait()
                link.step(dve.tensor_tensor(zr, ta, tb_, ALU.add))
                mul(ta, abi, ar)
                mul(tb_, nr, ai)
                mul(zr, zr, den)
                link.wait()
                link.step(dve.tensor_tensor(zi, ta, tb_, ALU.subtract))
                dve.tensor_tensor(zi, zi, den, ALU.mult).then_inc(z_ready, 1)
                dve.wait_ge(z_ready, 1)
                link.mark(dve.tensor_scalar(cmat[:, 2], cmat[:, 0], -1.0, None, ALU.mult))
                link.step(dve.tensor_scalar(cmat[:, 1], cmat[:, 1], -1.0, None, ALU.mult))
                for a, z in enumerate((zr, zi)):
                    dve.tensor_copy(zx[:, a], z.unsqueeze(2).to_broadcast([P, S5T, 32])).then_inc(c_ready, 1)
                for tab, m0, size in ((fine, 0, FINE), (middle, 5, 4), (top, 7, 4)):
                    link.mark(dve.memset(tab[:, 0, :, 0:1], 1.0))
                    link.step(dve.memset(tab[:, 1, :, 0:1], 0.0))
                    w, m = 1, m0
                    while w < size:
                        base = [b[:, m, :].unsqueeze(2).to_broadcast([P, S5T, w]) for b in (co, si)]
                        tmp = [ph[:, 0, a, 0:S5T * w].rearrange("p (t w) -> p t w", w=w) for a in range(4)]
                        cmul([tab[:, a, :, w:2 * w] for a in range(2)], [tab[:, a, :, 0:w] for a in range(2)], base, tmp)
                        w, m = 2 * w, m + 1
                dve.wait_ge(z_psum, 1)
                zre, zim = (lp[:, 2 * a:2 * a + 2, :].rearrange("p b (k d) -> p (b k) d", d=P) for a in range(2))
                mul(bbar[:, 0], zre, braw[:, 0])
                mul(bprod[:, 0], zim, braw[:, 1])
                mul(bbar[:, 1], zre, braw[:, 1])
                mul(bprod[:, 1], zim, braw[:, 0])
                link.wait()
                dve.tensor_tensor(bbar[:, 0], bbar[:, 0], bprod[:, 0], ALU.subtract).then_inc(bbar_ready, 1)
                dve.tensor_tensor(bbar[:, 1], bbar[:, 1], bprod[:, 1], ALU.add).then_inc(bbar_ready, 1)
                def sample_states():
                    dve.wait_ge(sbu_ready, 1)
                    ab = [a.unsqueeze(2).to_broadcast([P, S5T, NS]) for a in (abr, abi)]
                    tmp = [stmp[:, a, :].rearrange("p (t n) -> p t n", n=NS) for a in range(4)]
                    cmul([s5h[:, a] for a in range(2)], [s5s[:, a] for a in range(2)], ab, tmp)
                    sbu = lp[:, 0, :].rearrange("p (k a m) -> p k a m", a=2, m=4 * NS)
                    for a in range(2):
                        h4 = s5h[:, a].rearrange("p (k j) n -> p k (j n)", j=4)
                        dve.tensor_tensor(h4, h4, sbu[:, :, a, :], ALU.add).then_inc(s5h_ready, 1)

                def first_angles(t, s, first=False):
                    if not first:
                        dve.wait_ge(ph_dve, t * 2 - 2)
                        dve.wait_ge(ph_pool, t * 2 - 2)
                    f4, c4 = ([tab[:, a, bass.ds(t, 1), :].rearrange("p o b -> p (o b)") for a in range(2)]
                              for tab in (fine, middle))
                    f4 = [a.unsqueeze(1).to_broadcast([P, 4, FINE]) for a in f4]
                    c4 = [a.unsqueeze(2).to_broadcast([P, 4, FINE]) for a in c4]
                    v = lambda a: a.rearrange("p (a b) -> p a b", b=FINE)
                    out = [v(rot[:, s, a, 0:P]) for a in range(2)]
                    tmp = [v(rtmp[:, a, 0:P]) for a in range(2)]
                    pr = [out[0], tmp[0], out[1], tmp[1]]
                    for q, (a, b) in enumerate(((0, 0), (1, 1), (1, 0), (0, 1))):
                        mul(pr[q], f4[a], c4[b])
                    link.wait()
                    for a in range(2):
                        dve.tensor_tensor(out[a], out[a], tmp[a], (ALU.subtract, ALU.add)[a]).then_inc(first_ready, 1)

                def other_angles(t, s):
                    for a in range(2):
                        dve.wait_ge(spun_ready, t * 4 + 2 * a + 2)
                        dve.tensor_tensor(rot[:, s, a, P:NP_].rearrange("p (a b) -> p a b", b=P), spun[:, 2 * a], spun[:, 2 * a + 1],
                                          (ALU.subtract, ALU.add)[a]).then_inc(rot_ready, 1)
                    dve.wait_ge(rot_ready, t * 2 + 2)

                def turn_in(t, s, then):
                    dve.wait_ge(bu_ready, t + 1)
                    dve.wait_ge(u_ready, t * 2)
                    for a, (cs, b) in enumerate(((0, 0), (1, 1), (0, 1), (1, 0))):
                        dve.tensor_tensor(turned[:, a, :], rot[:, s, cs, :], mb[:, 2 * s + b, :], ALU.mult
                                          ).then_inc(turned_ready, 1)
                        if a == 1:
                            then()

                def scan(t, s, first=False):
                    dve.wait_ge(ph_dve, t * 2)
                    dve.wait_ge(ph_pool, t * 2)
                    decay = mag[:, bass.ds(t, 1)].to_broadcast([P, NP_])
                    for a in range(2):
                        dve.wait_ge(u_ready, t * 2 + (a + 1))
                        dve.tensor_tensor_scan(gst[:, a, :], decay, uin[:, a, :], 0.0, ALU.mult, ALU.add
                                               ).then_inc(g_ready, 1)
                    if not first:
                        dve.wait_ge(y_done, t - 1)
                        dve.wait_ge(fin_ready, t * 2 - 2)
                    dve.wait_ge(g_ready, t * 2 + 1)
                    for a in range(2):
                        dve.tensor_tensor(ph[:, s, a, :], rot[:, s, a, :], gst[:, 0, :], ALU.mult).then_inc(ph_dve, 1)

                def skip(k, b):
                    dve.wait_ge(y_done, k * 4 + 4)
                    dve.wait_ge(syc_ready, 1)
                    xk = x[:, bass.ds(k, 1), :].rearrange("p o n -> p (o n)")
                    mk = mixC[:, bass.ds(k, 1), :].rearrange("p o n -> p (o n)")
                    dk = s5d[:, bass.ds(k, 1)]
                    dve.scalar_tensor_tensor(mk[:, 0:NP_], xk[:, 0:NP_], dk, lp[:, 1 + b, :], ALU.mult, ALU.add
                                             ).then_inc(gin_ready, 1)
                    dve.scalar_tensor_tensor(mk[:, NP_:N], xk[:, NP_:N], dk, lp[:, 3, bass.ds(k * NS, NS)],
                                             ALU.mult, ALU.add).then_inc(gin_ready, 1)

                first_angles(0, 0, True)
                other_angles(0, 0)
                turn_in(0, 0, lambda: first_angles(1, 1, True))
                for t in range(1, 4):
                    scan(t - 1, (t - 1) % 2, t < 3)
                    other_angles(t, t % 2)
                    turn_in(t, t % 2, lambda: first_angles(t + 1, (t + 1) % 2))
                    if t == 1:
                        sample_states()

                def quad(k, b, last=False):
                    for j in range(4):
                        scan(k * 4 + (j - 1), (j - 1) % 2)
                        other_angles(k * 4 + j, j % 2)
                        turn_in(k * 4 + j, j % 2,
                                lambda: first_angles(k * 4 + (j + 1), (j + 1) % 2) if j < 3 or not last else None)
                        if j == 2:
                            skip(k - 1, b)

                quad(1, 0)
                with dve.Fori(0, KT // 2 - 2) as i:
                    link.loop(i, 32)
                    quad(i * 2 + 2, 1)
                    quad(i * 2 + 3, 0)
                    link.end(KT // 2 - 2)
                quad(KT - 2, 1)
                quad(KT - 1, 0, last=True)
                scan(S5T - 1, (S5T - 1) % 2)
                skip(KT - 1, 1)
                for m in range(KT):
                    dve.wait_ge(tile_out, t0 + 2 * m + 2)
                    val, gate = lw[:, 4 + m % 2, :], lw[:, 6 + m % 2, :]
                    link.step(dve.tensor_tensor(val, val, gate, ALU.mult))
                    dve.scalar_tensor_tensor(r[:, m, :], x[:, m, :], ALPHA, val, ALU.mult, ALU.add).then_inc(glu_done, 1)
                    dve.wait_ge(glu_done, m + 1)
                    add_sum(m)
            else:
                dve.wait_ge(tile_out, ttail)
                for m in range(KT):
                    residual(tail + m, ttail + m, m, "whole")
            norm(ln, y)
            for half in range(2):
                t1 = y["tm"] + 24 * half
                g1 = HHALF * (2 * y["i"] + half)
                with dve.Fori(0, HHALF // 4) as i:
                    link.loop(i, 8)
                    for c in range(4):
                        dve.wait_ge(tile_out, i * 4 + (t1 + c + 1))
                        hq = lw[:, 4 + c % 2, :]
                        m = i * 4 + c
                        hi = hh[:, bass.ds(m, 1), :].rearrange("p o n -> p (o n)")
                        lo = hl[:, bass.ds(m, 1), :].rearrange("p o n -> p (o n)")
                        link.step(dve.tensor_tensor(hq, lw[:, 6 + c % 2, :], lw[:, 6 + c % 2, :], ALU.mult))
                        link.step(dve.tensor_copy(hi, hq))
                        dve.tensor_tensor(lo, hq, hi.bitcast(F32), ALU.subtract).then_inc(h_ready, 1)
                        dve.wait_ge(h_ready, i * 4 + (g1 + c + 1))
                    link.end(HHALF // 4)
                dve.wait_ge(tile_out, t1 + HHALF)
                for m in range(KT):
                    residual(y["cm"] + 32 * half + HHALF + 2 * m + 1, t1 + HHALF + m, m, ("first", "second")[half])
            norm(ln + 1, y)

    @block.tensor
    def _(pe):
        def bank(T, half):
            b = 2 * (T % 2) + half
            return lp[:, b, 0:NH2]

        def chunk(n, slot, T, hi, lo, k0, start, stop, split=None, ks=range(KT)):
            if 0 in ks:
                pe.wait_ge(w_low, n + 1)
            for k in ks:
                if split is not None:
                    pe.wait_ge(xl_ready, split + k + 1)
                w = slice(k * P, (k + 1) * P)
                for half in range(2):
                    t = slice(half * NH2, (half + 1) * NH2)
                    first, last = start and k == 0, stop and k == KT - 1
                    pe.matmul(bank(T, half), wh[:, slot, w], hi[:, k0 + k, t], start=first, stop=False)
                    pe.matmul(bank(T, half), wh[:, slot, w], lo[:, k0 + k, t], start=False, stop=False)
                    ins = pe.matmul(bank(T, half), wl[:, slot, w], hi[:, k0 + k, t], start=False, stop=last)
            return ins

        def tile(n, T, split=None):
            if T >= 2:
                pe.wait_ge(tile_out, T - 1)
            chunk(n, n % SPL, T, xh, xl, 0, True, True, split).then_inc(chunk_done, 1)

        def part(n, T, ks, split=None):
            if 0 in ks and T >= 2:
                pe.wait_ge(tile_out, T - 1)
            ins = chunk(n, n % SPL, T, xh, xl, 0, True, True, split, ks)
            if KT - 1 in ks:
                ins.then_inc(chunk_done, 1)

        def pair(n, T, split, ks=range(KT)):
            for k in ks:
                part(n, T, (k,), split)
                part(n + 1, T + 1, (k,), split)

        def stats(ln, ready, n):
            def means(b, src, first):
                for half in range(2):
                    ins = pe.matmul(mb[:, b + half, 0:NH2], ones_mean[:], src[:, half * NH2:(half + 1) * NH2],
                                    start=first, stop=not first)
                return ins

            pe.wait_ge(sum_ready, ln + 1)
            means(0, rsum, True)
            pe.wait_ge(sq_added, 7 * (ln + 1))
            means(2, rsq, True)
            pe.wait_ge(ready, n)
            means(0, r[:, KT - 1, :], False)
            pe.wait_ge(sq_ready, 8 * (ln + 1))
            means(2, lw[:, 2 + (KT - 1) % 2, :], False).then_inc(stats_ready, 1)

        def hgrn_head(G, h, dense):
            p = h % 2
            k_, q_, v_ = (fq[:, 4 * p + a, :] for a in (1, 2, 3))
            ct = [slice(c * P, (c + 1) * P) for c in range(TB)]
            pe.wait_ge(kp_ready, G + 1)
            if G:
                pe.wait_ge(osq_ready, G)
                pe.wait_ge(orstd_ready, G)
            for c in range(TB):
                pe.transpose(mb[:, 0, ct[c]], kp[:, ct[c]], ident[:])
                pe.transpose(mb[:, 1, ct[c]], v_[:, ct[c]], ident[:])
            pe.transpose(mb[0:NS, 2, 0:P], k_[:, NP_:N], ident[:])
            pe.transpose(mb[0:NS, 2, P:2 * P], v_[:, NP_:N], ident[:]).then_inc(tok_ready, 1)
            pe.wait_ge(qt_ready, 8 * G + 1)
            for c in range(TB):
                ins = pe.matmul(mb[:, 3, ct[c]], k_[:, ct[c]], q_[:, ct[c]], start=True, stop=True)
            ins.then_inc(att_ready, 1)
            dense(2, (6, 7))
            for l in range(1, LEVELS + 1):
                pe.wait_ge(kt_ready, 7 * G + l)
                pe.wait_ge(qt_ready, 8 * G + l + 1)
                if l == 1:
                    pe.wait_ge(tok_copied, 3 * (G + 1))
                else:
                    pe.wait_ge(att_merged, 8 * G + l - 1)
                for c in range(TB):
                    q2 = slice(c * P // 2, (c + 1) * P // 2)
                    ins = pe.matmul(mb[:, 2 if l % 2 else 3, q2], kt[:, l - 1, ct[c]], qt[:, l - 1, q2],
                                    start=True, stop=True)
                ins.then_inc(att_ready, 1)
                if l < LEVELS:
                    dense(3, (l - 1,))
            for c in range(TB):
                ins = pe.matmul(mb[:, 1, ct[c]], ktok[:, ct[c]], vtok[:, ct[c]], start=True, stop=True)
            ins.then_inc(upd_ready, 1)
            pe.wait_ge(vz_ready, G + 1)
            pe.wait_ge(att_merged, 8 * G + 8)
            for b in range(2):
                ins = pe.matmul(mb[:, 2 + b, :], tok8[:, 0, :], vz[:, 4 * b:4 * b + 4, :].rearrange("k n d -> k (n d)"),
                                start=True, stop=True)
            ins.then_inc(su_ready, 1)
            pe.wait_ge(states_ready, G + 1)
            for c in range(TB):
                ins = pe.matmul(mb[:, 0, ct[c]], vtok[:, ct[c]], att[:, ct[c]], start=True, stop=c == 0)
                if c:
                    ins = pe.matmul(mb[:, 0, ct[c]], st[:, c - 1, :], qe[:, ct[c]], start=False, stop=True)
            ins.then_inc(o_ready, 1)
            pe.wait_ge(snew_ready, G + 1)
            for n in range(NS):
                ins = pe.matmul(mb[:, 1, n:n + 1], s0b[:, G % 2, n, :], q_[:, NP_ + n:NP_ + n + 1], start=True, stop=True)
            ins.then_inc(so_ready, 1)
            dense(3, (6,))
            pe.wait_ge(osq_ready, G + 1)
            for b in range(2):
                ins = pe.matmul(mb[:, 2 + b, 0:NH2], ones_head[:], osq[:, b * NH2:(b + 1) * NH2], start=True, stop=True)
            ins.then_inc(ms_ready, 1)
            dense(3, (7,))

        def dsa(y, c0, t0):
            pair(c0, t0, 8 * 3 * y["i"])
            pe.wait_ge(ki_raw, 1)
            pe.wait_ge(b_loaded, 16 * 8)
            for b in range(2):
                pe.matmul(mb[:, b, 0:NH2], ones_idx[:], kiT[:, b * NH2:(b + 1) * NH2], start=True, stop=True)
            for b in range(2):
                ins = pe.matmul(mb[:, 2 + b, 0:NH2], ones_idx[:], rl[:, 0, b * NH2:(b + 1) * NH2], start=True, stop=True)
            ins.then_inc(ki_stats, 1)
            for c in range(2, 5):
                tile(c0 + c, t0 + c)
            pe.wait_ge(ki_var, 1)
            pe.wait_ge(x_ready, 16 * y["i"])
            for qb in range(1, TB):
                for k in range(KT):
                    pe.matmul(mb[:, 0, (qb - 1) * IH:qb * IH], x[:, k, qb * P:(qb + 1) * P], wwi[:, k, :],
                              start=k == 0, stop=k == KT - 1)
            for a in range(2):
                for k in range(KT):
                    ins = pe.matmul(mb[0:4, 1, a * NS:(a + 1) * NS], wwi[:, k, 4 * a:4 * a + 4], x[:, k, NP_:N],
                                    start=k == 0, stop=k == KT - 1)
            ins.then_inc(wi_psum, 1)
            pe.matmul(mb[0:HEADS, 2, :], relb[:, 0:8], oh_p[:, 0:512], start=True, stop=True)
            pe.matmul(mb[0:HEADS, 3, 0:ROW - 512], relb[:, 0:8], oh_p[:, 512:ROW], start=True, stop=True
                      ).then_inc(rows_ready, 1)
            tile(c0 + 5, t0 + 5)
            tile(c0 + 6, t0 + 6)
            pe.wait_ge(ki_ready, 1)
            pe.wait_ge(rows_out, 2)
            for u, (qb, h) in enumerate(IUNITS):
                w = (qb + 1) * P
                half = slice(64 * (h % 2), 64 * (h % 2) + 64)
                if u < 4:
                    pe.wait_ge(wi_ready, 2)
                else:
                    pe.wait_ge(relu_done, u - 3)
                pe.matmul(mb[:, u % 4, 0:w], qi[half, h // 2, qb * P:(qb + 1) * P], kiT[half, 0:w], start=True, stop=True
                          ).then_inc(dot_ready, 1)
            pe.wait_ge(relu_done, len(IUNITS))
            pe.wait_ge(w3_ready, 2)
            for n in range(NS):
                pe.wait_ge(kx_loaded[n % 2], 32 * (n // 2 + 1))
                pe.wait_ge(kx_own, n + 1)
                if n:
                    pe.wait_ge(srelu_done, n)
                for a in range(2):
                    half = slice(64 * a, 64 * a + 64)
                    ins = pe.matmul(mb[0:4, a, 0:SK], qi[half, :, NP_ + n], kx[half, n % 2, :], start=True, stop=True)
                ins.then_inc(sdot_ready, 1)
                pe.wait_ge(srelu_done, n + 1)
                for a in range(2):
                    ins = pe.matmul(mb[0:NS, 2, 0:SK], w3[:, a, n, :], srl[:, a, :], start=n == 0 and a == 0,
                                    stop=n == NS - 1 and a == 1)
                ins.then_inc(s8_ready, 1)
            for c in range(7, 29):
                tile(c0 + c, t0 + c)
                if c >= 14 and c % 2 == 0:
                    n = (c - 14) // 2
                    pe.wait_ge(pg_loaded[n % 2], 32 * (n // 2 + 1))
                    pe.wait_ge(tile_out, t0 + 13)
                    for g in range(2):
                        for h in range(HEADS):
                            col = g * HN + h * NS + n
                            ins = pe.matmul(mb[:, 3, col:col + 1], pg[:, n % 2, g, h * P:(h + 1) * P],
                                            mixB[:, h, NP_ + n:NP_ + n + 1], start=True, stop=True)
                    ins.then_inc(pages_used, 1)
                if c >= 22:
                    turn_values(c - 22, t0)
            turn_values(HEADS - 1, t0)
            pe.wait_ge(vtr_out, HEADS)
            pe.wait_ge(tile_out, t0 + 29)
            pe.wait_ge(sprod, 1)
            pe.matmul(mb[0:HN, 1, PAST:SK], sprodt, ones[:, 0:1], start=True, stop=True).then_inc(spsum, 1)
            pe.wait_ge(slog, 1)
            for g in range(2):
                ins = pe.transpose(mb[0:HN, 1, g * P:(g + 1) * P], ltok[:, g * HN:(g + 1) * HN], ident[:])
            ins.then_inc(sy_ready, 1)
            pe.wait_ge(sneg_ready, 1)
            pe.matmul(mb[0:HN, 2, 0:SK], relb[:, 8:72], oh_p[:, ROW:ROW + SK], start=True, stop=False)
            pe.matmul(mb[0:HN, 2, 0:SK], rep8, s8, start=False, stop=True).then_inc(sz_ready, 1)
            pe.wait_ge(sp_ready, 1)
            for g in range(2):
                pe.transpose(mb[:, 3, g * HN:(g + 1) * HN], sl[:, g * P:(g + 1) * P], ident[0:HN, 0:HN])
            pe.matmul(mb[:, 1, 0:HN], ones[0:HN, :], sdiag, start=True, stop=True).then_inc(spt_ready, 1)
            pe.wait_ge(spt_out, 1)
            def logits(u):
                h, qb = UNITS[u]
                w = (qb + 1) * P
                if u >= 2:
                    pe.wait_ge(l_ready, u - 1)
                pe.matmul(mb[:, u % 2, 0:w], mixB[:, h, qb * P:(qb + 1) * P], kT[:, h, 0:w], start=True, stop=True
                          ).then_inc(log_ready, 1)

            def turn(u):
                h, qb = UNITS[u]
                pe.wait_ge(p_ready, u + 1)
                if u >= 2:
                    pe.wait_ge(ptr_out, u - 1)
                for s in range(qb + 1):
                    ins = pe.transpose(mb[:, 2 + u % 2, s * P:(s + 1) * P], pb_[:, u % 2, s * P:(s + 1) * P], ident[:])
                ins.then_inc(ptr_ready, 1)

            def values(u):
                h, qb = UNITS[u]
                pe.wait_ge(ptr_out, u + 1)
                if qb == 0 and h >= 2:
                    pe.wait_ge(pv_out, h - 1)
                for s in range(qb + 1):
                    ins = pe.matmul(lp[:, h % 2, qb * P:(qb + 1) * P], vtk[:, s, h, :], pt_[:, u % 2, s * P:(s + 1) * P],
                                    start=s == 0, stop=s == qb)
                ins.then_inc(pv_ready, 1)

            def page_values(n):
                slot = (NS + n) % 2
                pe.wait_ge(pg_loaded[slot], 32 * ((NS + n) // 2 + 1))
                for h in range(HEADS):
                    col = h * NS + n
                    for g in range(2):
                        ins = pe.matmul(lp[:, 2, col:col + 1], pg[:, slot, g, h * P:(h + 1) * P],
                                        sptt[:, g * HN + col:g * HN + col + 1], start=g == 0, stop=g == 1)
                ins.then_inc(pages_used, 1)

            pe.wait_ge(sbc_out, 1)
            logits(0)
            logits(1)
            for u in range(len(UNITS)):
                if u + 2 < len(UNITS):
                    logits(u + 2)
                turn(u)
                if u:
                    values(u - 1)
                if u % TB == TB - 1:
                    page_values(u // TB)
            values(len(UNITS) - 1)

        def turn_values(h, t0):
            pe.wait_ge(tile_out, t0 + 21 + h + 1)
            if h >= 2:
                pe.wait_ge(vtr_out, h - 1)
            elif h == 0:
                pe.wait_ge(s8_out, 1)
            for b in range(TB):
                ins = pe.transpose(mb[:, h % 2, b * P:(b + 1) * P], vT[:, h % 2, b * P:(b + 1) * P], ident[:])
            ins.then_inc(vtr_ready, 1)

        pe.wait_ge(consts_set, 7)
        pe.wait_ge(const_loaded, 64)
        for y in plan:
            ln = 2 * y["i"]
            c0, t0 = y["c"], y["t"]
            if y["kind"] == 0:
                g0 = 8 * y["j"]
                for h in range(HEADS + 1):
                    def dense(j, ks):
                        if h < HEADS:
                            part(c0 + 4 * h + j, t0 + 4 * h + j, ks)
                        elif j == 3 and ks[-1] < KT - 1:
                            pair(c0 + 32, t0 + 32, 8 * (3 * y["i"] + 1), ks)

                    if h == 0:
                        pair(c0, t0, 8 * 3 * y["i"])
                        for j in range(2, 4):
                            tile(c0 + j, t0 + j)
                    else:
                        dense(0, range(KT))
                        dense(1, range(KT))
                        dense(2, range(6))
                        hgrn_head(g0 + h - 1, h - 1, dense)
                tail, ttail = c0 + 32, t0 + 32
            if y["kind"] == 1:
                dsa(y, c0, t0)
                tail, ttail = c0 + 29, t0 + 29
            if y["kind"] == 2:
                pe.wait_ge(x_ready, 16 * y["i"])
                for s in x_loaded:
                    pe.wait_ge(s, 16)
                pe.wait_ge(tile_out, t0)
                pe.wait_ge(c_ready, 2)
                for a in range(2):
                    for k in range(KT):
                        zcol = zx[:, a, 4 * k:4 * k + 4, :].rearrange("p t f -> p (t f)")
                        ins = pe.matmul(lp[:, 2 * a + k // 4, (k % 4) * P:(k % 4 + 1) * P], zcol, ident[:], start=True, stop=True)
                ins.then_inc(z_psum, 1)
                pe.wait_ge(bbar_ready, 2)
                def inputs(t):
                    k, f = t // 4, slice(32 * (t % 4), 32 * (t % 4) + 32)
                    if t >= 2:
                        pe.wait_ge(turned_ready, 4 * (t - 1))
                    for a in range(2):
                        ins = pe.matmul(mb[:, 2 * (t % 2) + a, :], bbar[f, a, k, :], x[f, k, 0:NP_], start=True, stop=True,
                                        tile_position=(32 * (t % 4), 0))
                    ins.then_inc(bu_ready, 1)

                def outputs(t):
                    k, f = t // 4, slice(32 * (t % 4), 32 * (t % 4) + 32)
                    if t % 4 == 0 and k >= 2:
                        pe.wait_ge(gin_ready, 2 * (k - 1))
                    pe.wait_ge(ph_dve, 2 * t + 2)
                    for n, (a, b) in enumerate(((0, 0), (1, 1), (2, 2), (1, 3))):
                        if n == 2:
                            pe.wait_ge(ph_pool, 2 * t + 2)
                        ins = pe.matmul(lp[f, 1 + k % 2, :], cmat[:, a, t, :], ph[:, t % 2, b, :], start=n == 0, stop=n == 3,
                                        tile_position=(0, 32 * (t % 4)))
                    ins.then_inc(y_done, 1)

                def sample_outputs(k):
                    for t in range(4 * k, 4 * k + 4):
                        f = slice(32 * (t % 4), 32 * (t % 4) + 32)
                        for a in range(2):
                            ins = pe.matmul(lp[f, 3, k * NS:(k + 1) * NS], cmat[:, a, t, :], s5h[:, a, t, :],
                                            start=a == 0, stop=a == 1, tile_position=(0, 32 * (t % 4)))
                    if k == KT - 1:
                        ins.then_inc(syc_ready, 1)

                inputs(0)
                inputs(1)
                pe.wait_ge(x4_ready, 5)
                for k in range(KT):
                    for a in range(2):
                        ins = pe.matmul(lp[:, 0, (2 * k + a) * 32:(2 * k + a + 1) * 32], bbar[:, a, k, :],
                                        x4[:, k, :, :].rearrange("p j n -> p (j n)"), start=True, stop=True)
                ins.then_inc(sbu_ready, 1)

                pe.wait_ge(s5h_ready, 2)
                for t in range(S5T):
                    outputs(t)
                    if t + 2 < S5T:
                        inputs(t + 2)
                    if t < 4:
                        sample_outputs(2 * t)
                        sample_outputs(2 * t + 1)
                pe.wait_ge(gin_ready, 2 * KT)
                pair(c0, t0, 8 * (3 * y["i"] + 1))
                for m in range(2, 2 * KT):
                    tile(c0 + m, t0 + m)
            else:
                pair(tail, ttail, 8 * (3 * y["i"] + 1), (KT - 1,) if y["kind"] == 0 else range(KT))
                for m in range(2, KT):
                    tile(tail + m, ttail + m)
            stats(ln, *((glu_done, KT) if y["kind"] == 2 else (tile_out, ttail + KT)))
            for half in range(2):
                c1, t1 = y["cm"] + 32 * half, y["tm"] + 24 * half
                s0_ = 0
                if half == 0:
                    pair(c1, t1, 8 * (3 * y["i"] + 2))
                    s0_ = 1
                g1 = HHALF * (2 * y["i"] + half)
                if half == 0:
                    for c in range(2, 4):
                        tile(c1 + c, t1 + c)
                    lo_, hi_ = 1, HHALF // 4
                else:
                    lo_, hi_ = 0, HHALF // 4
                with pe.Fori(lo_, hi_) as i:
                    for c in range(4):
                        T = t1 + c
                        pe.wait_ge(tile_out, i * 4 + T - 1)
                        chunk(i * 4 + (c1 + c), (c1 + c) % SPL, T, xh, xl, 0, True, True).then_inc(chunk_done, 1)
                c2, t2 = c1 + HHALF, t1 + HHALF
                pe.wait_ge(h_ready, g1 + HHALF)
                with pe.Fori(0, KT // 2) as i:
                    for m in range(2):
                        T = t2 + m
                        pe.wait_ge(tile_out, i * 2 + T - 1)
                        for b in range(2):
                            n = c2 + 2 * m + b
                            ins = chunk(i * 4 + n, n % SPL, T, hh, hl, 8 * b, b == 0, b == 1)
                            ins.then_inc(chunk_done, 1)
            stats(ln + 1, tile_out, y["tm"] + MLP_TILES)

    ctx.close()


def t5_bucket(rel):
    n = np.maximum(rel, 0)
    exact = REL // 2
    nf = np.maximum(n, exact).astype(np.float32)
    large = exact + (np.log(nf / np.float32(exact)) / np.float32(math.log(128 / exact)) * np.float32(REL - exact)
                     ).astype(np.int32)
    return np.where(n < exact, n, np.minimum(large, REL - 1))


def layouts(i):
    def chunks(w):
        k, m = w.shape
        return np.ascontiguousarray(w.reshape(k // D, KT, P, m // P, P).transpose(3, 0, 2, 1, 4)
                                    ).reshape(m // P, k // D, P, KT * P)

    def cols(a):
        return np.ascontiguousarray(np.moveaxis(a.reshape(a.shape[:-1] + (KT, P)), -1, 0))

    stream, occ = [], [0, 0, 0]
    for l, kind in enumerate(KINDS):
        j = occ[kind]
        occ[kind] += 1
        if kind == 0:
            c = chunks(i["hg_w_in"][j])[:, 0]
            q, f, v, g = (c[8 * a:8 * a + 8] for a in range(4))
            for h in range(HEADS):
                stream += [f[h], q[h], v[h], g[h]]
            stream += list(chunks(i["hg_w_out"][j])[:, 0])
        if kind == 1:
            w = i["dsa_w_in"][j]
            hd, iq = HEADS * DH, IH * IDX_DIM
            ki = w[:, 3 * hd + iq:3 * hd + iq + IDX_DIM]
            stream += list(chunks(np.concatenate([ki, ki], axis=1))[:, 0])
            stream += list(chunks(w[:, 3 * hd:3 * hd + iq])[:, 0])
            for a in range(3):
                stream += list(chunks(w[:, a * hd:(a + 1) * hd])[:, 0])
            stream += list(chunks(i["dsa_w_out"][j])[:, 0])
        if kind == 2:
            c = chunks(i["s5_w_glu"][j])[:, 0]
            for m in range(KT):
                stream += [c[m], c[KT + m]]
        c1, c2 = chunks(i["mlp_w1"][l])[:, 0], chunks(i["mlp_w2"][l])
        for half in range(2):
            stream += list(c1[HHALF * half:HHALF * (half + 1)])
            for m in range(KT):
                stream += [c2[m, 2 * half], c2[m, 2 * half + 1]]
    out = {"wstream": np.stack(stream)}
    xs = np.concatenate([i["x_prompt"].reshape(NP_, D), i["x_sample"].reshape(NS, D)])
    out["xT"] = np.ascontiguousarray(xs.T.reshape(KT, P, N).transpose(1, 0, 2))
    out["ident"] = np.eye(P, dtype=np.float32)
    out["lnp"] = np.stack([cols(i[k]) for k in ("ln_mix_g", "ln_mix_b", "ln_ffn_g", "ln_ffn_b")], axis=1)
    out["hgp"] = cols(i["hg_gnorm"])
    out["lbp"] = cols(i["hg_lb"])
    out["s_in"] = i["state_hgrn"]
    w = i["dsa_w_in"][0][:, 3 * HEADS * DH + IH * IDX_DIM + IDX_DIM:]
    w = w[:, [0, 2, 4, 6, 1, 3, 5, 7]]
    out["wwi"] = np.ascontiguousarray(w.reshape(KT, P, IH).transpose(1, 0, 2))
    out["kiln"] = np.stack([np.tile(i["dsa_kln_g"][0], 2), np.tile(i["dsa_kln_b"][0], 2)], axis=1)
    out["ones_idx"] = np.kron(np.eye(2), np.full((64, 64), 1 / 64)).astype(np.float32)
    q, k = np.arange(P)[:, None], np.arange(P)[None, :]
    out["cmask"] = np.where(k <= q, 0, NEG).astype(np.float32)
    out["page_table"] = i["page_table"].reshape(1, 2 * NS)
    kidx = i["cache_kidx"][0].transpose(0, 2, 1)
    out["kidxT"] = np.concatenate([kidx, kidx], axis=1)
    out["kpages"] = np.ascontiguousarray(i["cache_k"][0].transpose(0, 3, 2, 1)).reshape(-1, DH, D)
    out["vpages"] = i["cache_v"][0].reshape(-1, P, D)
    rb = i["rel_bias"]
    out["relb"] = np.concatenate([rb, np.repeat(rb, NS, axis=1)], axis=1)
    rel = np.concatenate([NP_ - 1 - np.arange(ROW), PAST - np.arange(SK)])
    out["oh_p"] = (t5_bucket(rel)[None, :] == np.arange(REL)[:, None]).astype(np.float32)
    out["rep8"] = np.tile(np.eye(NS, dtype=np.float32), (1, HEADS))
    out["oh4"] = np.tile(np.eye(NS, dtype=np.float32).reshape(1, -1), (4, 1))
    def by_state(a):
        a = a.reshape((S5T, P) + a.shape[2:])
        return np.ascontiguousarray(a.swapaxes(0, 1))

    def blocks(a):
        b = np.zeros((S5T, 2, 16, 2, 64), np.float32)
        a = a.reshape(S5T, 2, 64, 16)
        for g in range(2):
            b[:, g, :, g, :] = a[:, g].transpose(0, 2, 1)
        return b.reshape(S5T, 32, P)

    ldt = np.broadcast_to(i["s5_log_dt"][0][:, None], (64, 64))
    out["s5_ab"] = np.stack([by_state(a) for a in (i["s5_a_re"][0], i["s5_a_im"][0], ldt)], axis=1)
    out["s5_b"] = np.stack([blocks(i[k][0]).reshape(KT, P, P).transpose(1, 0, 2) for k in ("s5_b_re", "s5_b_im")], axis=1)
    out["s5_c"] = np.stack([blocks(i[k][0].swapaxes(1, 2)).transpose(2, 0, 1) for k in ("s5_c_re", "s5_c_im")], axis=1)
    out["s5_s"] = np.stack([by_state(i[k][0].transpose(1, 2, 0)) for k in ("state_s5_re", "state_s5_im")], axis=1)
    out["s5_d"] = cols(i["s5_d"][0])
    out["s5_g"] = np.ascontiguousarray(i["s5_b_glu"][0].reshape(2 * KT, P).T)
    s = np.arange(P)[:, None]
    mask = np.zeros((P, LEVELS, TB, P // 2), np.int32)
    for l in range(LEVELS):
        m = 1 << l
        t = np.arange(P).reshape(-1, 2, m)[:, 1].reshape(-1)
        mask[:, l] = ((s // (2 * m) == t // (2 * m)) & (s % (2 * m) < m))[:, None, :]
    out["lmask"] = mask.reshape(P, LEVELS, TB * P // 2)
    return out


def token_major(a):
    return a.transpose(2, 1, 0).reshape(a.shape[2], -1)


OUTS = dict(yT=(P, KT, N), hg_p=(2, HEADS, P, P), hg_s=(2, NS, HEADS, P, P), kidxT=(IDX_DIM, N), kT=(P, KT, N),
            vT=(P, KT, N), s5_p=(P, 2, S5T), s5_s=(P, 2, S5T, NS))


def kernel(**inputs):
    import concourse.bacc as bacc
    from concourse.bass_utils import run_bass_kernel_spmd

    nc = bacc.Bacc("TRN2", target_bir_lowering=False, num_devices=1)
    arrays = {"in_" + n: np.ascontiguousarray(a) for n, a in layouts({k: np.asarray(v) for k, v in inputs.items()}).items()}
    I = {n[3:]: nc.dram_tensor(n, a.shape, mybir.dt.from_np(a.dtype), kind="ExternalInput").ap() for n, a in arrays.items()}
    O = {n: nc.dram_tensor("out_" + n, s, F32, kind="ExternalOutput").ap() for n, s in OUTS.items()}
    trunk(nc, I, O)
    res = run_bass_kernel_spmd(nc, [arrays], core_ids=[0]).results[0]
    y, k, v = (token_major(res["out_" + n]) for n in ("yT", "kT", "vT"))
    ki = res["out_kidxT"].T
    s5p = res["out_s5_p"].transpose(1, 2, 0).reshape(2, 1, 1, 64, 64)
    s5s = res["out_s5_s"].transpose(1, 3, 2, 0).reshape(2, 1, NS, 64, 64)
    return (y[:NP_].reshape(1, NP_, D), y[NP_:].reshape(NS, 1, D),
            res["out_hg_p"][:, None], res["out_hg_s"],
            k[:NP_].reshape(1, 1, NP_, HEADS, DH), v[:NP_].reshape(1, 1, NP_, HEADS, DH), ki[:NP_].reshape(1, 1, NP_, IDX_DIM),
            k[NP_:].reshape(1, NS, 1, HEADS, DH), v[NP_:].reshape(1, NS, 1, HEADS, DH), ki[NP_:].reshape(1, NS, 1, IDX_DIM),
            s5p[0], s5p[1], s5s[0], s5s[1])
```
